# Optimizing a Trainium2 kernel written in Bass

```python
import math
import jax, jax.numpy as jnp
from jax import lax
import numpy as np

D_MODEL = 1024
BATCH = 1
SEQ = 256
DEPTH = 2

GRID_W = 64
CTX_LEN = 256
N_MOD = 9
D_FF = 2816
EPS = 1e-6
ROPE_BASE = 10000.0
RET_WIDTH = D_MODEL // 2
RET_HEADS = 4
RET_HEAD_DIM = RET_WIDTH // RET_HEADS
RET_CHUNK = 128
S5_WIDTH = D_MODEL - RET_WIDTH
S5_GROUP = 16
S5_GROUPS = S5_WIDTH // S5_GROUP
S5_STATE = 64
S5_DT_MIN = 0.001
S5_DT_MAX = 0.1
AB_IN_WIDTH = 4 * RET_WIDTH + S5_WIDTH
NA_HEADS = 16
NA_HEAD_DIM = D_MODEL // NA_HEADS
NA_KH_MAX = 8
NA_KW = 16
NA_QBLOCK_W = 16
NA_KSPAN_W = 2 * NA_KW
NEG_INF = -1e30

kernel_name = "hybrid_retention_s5_natten_macaron_dit"

def rms_norm(x, g):
    xf = x.astype(jnp.float32)
    y = xf * lax.rsqrt(jnp.mean(xf * xf, axis=-1, keepdims=True) + EPS)
    return (y * g.astype(jnp.float32)).astype(x.dtype)

def modulate(x, g, shift, scale):
    return rms_norm(x, g) * (1 + scale) + shift

def swiglu(h, w1, w2):
    a, b = jnp.split(h @ w1, 2, axis=-1)
    return (jax.nn.silu(a) * b) @ w2

def axial_rope(x, row, col):
    dh = x.shape[-1]
    half = dh // 2
    quarter = half // 2
    inv = ROPE_BASE ** (-jnp.arange(0, half, 2, dtype=jnp.float32) / half)

    def rot(xp, pos):
        ang = pos.astype(jnp.float32)[:, None] * inv[None, :]
        cos = jnp.cos(ang)[None, :, None, :].astype(x.dtype)
        sin = jnp.sin(ang)[None, :, None, :].astype(x.dtype)
        x1, x2 = xp[..., :quarter], xp[..., quarter:]
        return jnp.concatenate([x1 * cos - x2 * sin, x2 * cos + x1 * sin], axis=-1)

    return jnp.concatenate([rot(x[..., :half], row), rot(x[..., half:], col)], axis=-1)

def retention_scan(q, k, v, log_gamma, s0):
    B, H, L, dk = q.shape
    dv = v.shape[-1]
    C = RET_CHUNK
    N = L // C
    qc = q.reshape(B, H, N, C, dk)
    kc = k.reshape(B, H, N, C, dk)
    vc = v.reshape(B, H, N, C, dv)
    pos = jnp.arange(C, dtype=jnp.float32)
    lg = log_gamma[:, None]
    diff = pos[:, None] - pos[None, :]
    dmask = jnp.where(diff >= 0, jnp.exp(lg[:, :, None] * jnp.maximum(diff, 0.0)), 0.0)
    inner = jnp.einsum('bhnid,bhnjd->bhnij', qc, kc) * dmask[None, :, None]
    o_inner = jnp.einsum('bhnij,bhnje->bhnie', inner, vc)
    k_w = jnp.exp(lg * (C - 1 - pos))
    kv = jnp.einsum('bhnjd,bhnje->nbhde', kc * k_w[None, :, None, :, None], vc)
    chunk_decay = jnp.exp(log_gamma * C)[None, :, None, None]

    def step(s, kv_n):
        return chunk_decay * s + kv_n, s

    s_final, s_prev = lax.scan(step, s0, kv)
    q_w = jnp.exp(lg * (pos + 1.0))
    o_cross = jnp.einsum('bhnid,nbhde->bhnie', qc * q_w[None, :, None, :, None], s_prev)
    return (o_inner + o_cross).reshape(B, H, L, dv), s_final

def retention_mixer(q_l, k_l, v_l, g_l, q_c, k_c, v_c, g_c, decay_logit, row, col, need_ctx):
    def heads(t):
        return t.reshape(t.shape[0], t.shape[1], RET_HEADS, RET_HEAD_DIM)

    def tr(t):
        return jnp.swapaxes(t, 1, 2).astype(jnp.float32)

    kscale = RET_HEAD_DIM ** -0.5
    ql = tr(axial_rope(heads(q_l), row, col))
    kl = tr(axial_rope(heads(k_l), row, col) * kscale)
    vl = tr(heads(v_l))
    qc = tr(heads(q_c))
    kc = tr(heads(k_c) * kscale)
    vc = tr(heads(v_c))
    log_gamma = jax.nn.log_sigmoid(decay_logit.astype(jnp.float32))
    s0 = jnp.zeros((q_l.shape[0], RET_HEADS, RET_HEAD_DIM, RET_HEAD_DIM), jnp.float32)

    def flip(t):
        return jnp.flip(t, axis=2)

    oc_f, sc_f = retention_scan(qc, kc, vc, log_gamma[0], s0)
    oc_b, sc_b = retention_scan(flip(qc), flip(kc), flip(vc), log_gamma[1], s0)
    ol_f, _ = retention_scan(ql, kl, vl, log_gamma[0], sc_f)
    ol_b, _ = retention_scan(flip(ql), flip(kl), flip(vl), log_gamma[1], sc_b)

    def finish(o, g):
        o = o * lax.rsqrt(jnp.mean(o * o, axis=-1, keepdims=True) + EPS)
        Bo, Ho, Lo, do = o.shape
        o = jnp.swapaxes(o, 1, 2).reshape(Bo, Lo, Ho * do)
        return (o * jax.nn.silu(g.astype(jnp.float32))).astype(g.dtype)

    y_l = finish(ol_f + flip(ol_b), g_l)
    y_c = finish(oc_f + flip(oc_b), g_c) if need_ctx else None
    return y_l, y_c

def _ssm_combine(e1, e2):
    a1, b1 = e1
    a2, b2 = e2
    return a1 * a2, a2 * b1 + b2

def ssm_scan(lam_bar, bu):
    a = jnp.broadcast_to(lam_bar, bu.shape)
    _, xs = lax.associative_scan(_ssm_combine, (a, bu), axis=1)
    return xs

def s5_mixer(u_lat, u_ctx, lam_re, lam_im, log_dt, b_re, b_im, c_re, c_im, d_skip, glu_w, glu_b, need_ctx):
    B, L, _ = u_lat.shape
    Lc = u_ctx.shape[1]
    ul = u_lat.astype(jnp.float32).reshape(B, L, S5_GROUPS, S5_GROUP)
    uc = u_ctx.astype(jnp.float32).reshape(B, Lc, S5_GROUPS, S5_GROUP)
    dsk = d_skip.astype(jnp.float32).reshape(S5_GROUPS, S5_GROUP)
    ys_l = dsk * ul
    ys_c = dsk * uc
    for direction in range(2):
        lam = lax.complex(jnp.minimum(lam_re[direction].astype(jnp.float32), -1e-4),
                          lam_im[direction].astype(jnp.float32))
        dt = jnp.exp(log_dt[direction].astype(jnp.float32))[:, None]
        lam_bar = jnp.exp(lam * dt)
        b_bar = ((lam_bar - 1.0) / lam)[..., None] * lax.complex(
            b_re[direction].astype(jnp.float32), b_im[direction].astype(jnp.float32))
        c_mat = lax.complex(c_re[direction].astype(jnp.float32), c_im[direction].astype(jnp.float32))
        if direction == 0:
            order = lambda t: t
        else:
            order = lambda t: jnp.flip(t, axis=1)
        bu_c = jnp.einsum('gpk,blgk->blgp', b_bar, order(uc).astype(jnp.complex64))
        x_c = ssm_scan(lam_bar, bu_c)
        bu_l = jnp.einsum('gpk,blgk->blgp', b_bar, order(ul).astype(jnp.complex64))
        bu_l = bu_l.at[:, 0].add(lam_bar * x_c[:, -1])
        x_l = ssm_scan(lam_bar, bu_l)
        ys_l = ys_l + order(jnp.einsum('gkp,blgp->blgk', c_mat, x_l).real)
        if need_ctx:
            ys_c = ys_c + order(jnp.einsum('gkp,blgp->blgk', c_mat, x_c).real)

    def glu(y, Ly):
        y = jax.nn.gelu(y.reshape(B, Ly, S5_WIDTH))
        y = y * jax.nn.sigmoid(y @ glu_w.astype(jnp.float32) + glu_b.astype(jnp.float32))
        return y.astype(u_lat.dtype)

    y_l = glu(ys_l, L)
    y_c = glu(ys_c, Lc) if need_ctx else None
    return y_l, y_c

def ab_mixer(h_lat, h_ctx, w_in, w_out, decay_logit, lam_re, lam_im, log_dt, b_re, b_im,
             c_re, c_im, d_skip, glu_w, glu_b, row, col, need_ctx):
    cuts = [RET_WIDTH, 2 * RET_WIDTH, 3 * RET_WIDTH, 4 * RET_WIDTH]
    ql, kl, vl, gl, ul = jnp.split(h_lat @ w_in, cuts, axis=-1)
    qc, kc, vc, gc, uc = jnp.split(h_ctx @ w_in, cuts, axis=-1)
    r_l, r_c = retention_mixer(ql, kl, vl, gl, qc, kc, vc, gc, decay_logit, row, col, need_ctx)
    s_l, s_c = s5_mixer(ul, uc, lam_re, lam_im, log_dt, b_re, b_im, c_re, c_im, d_skip, glu_w, glu_b, need_ctx)
    y_l = jnp.concatenate([r_l, s_l], axis=-1) @ w_out
    y_c = (jnp.concatenate([r_c, s_c], axis=-1) @ w_out) if need_ctx else None
    return y_l, y_c

def na_mixer(h_lat, h_ctx, w_qkv, w_o, rpb, need_ctx):
    B, S, _ = h_lat.shape
    rows = S // GRID_W
    kh = min(NA_KH_MAX, rows)
    H, dh = NA_HEADS, NA_HEAD_DIM
    scale = dh ** -0.5
    q, k, v = jnp.split(h_lat @ w_qkv, 3, axis=-1)
    qc, kc, vc = jnp.split(h_ctx @ w_qkv, 3, axis=-1)
    q_g = q.reshape(B, rows, GRID_W, H, dh) * scale
    k_g = k.reshape(B, rows, GRID_W, H, dh)
    v_g = v.reshape(B, rows, GRID_W, H, dh)
    k_c = kc.reshape(B, -1, H, dh)
    v_c = vc.reshape(B, -1, H, dh)
    n_cb = GRID_W // NA_QBLOCK_W
    row_start = jnp.clip(jnp.arange(rows) - kh // 2, 0, rows - kh)
    qcol = np.arange(GRID_W).reshape(n_cb, NA_QBLOCK_W)
    kcol0 = np.clip(np.arange(n_cb) * NA_QBLOCK_W - NA_KW // 2, 0, GRID_W - NA_KSPAN_W)
    kcol = kcol0[:, None] + np.arange(NA_KSPAN_W)
    wstart = np.clip(qcol - NA_KW // 2, 0, GRID_W - NA_KW)
    kc3 = kcol[:, None, :]
    col_valid = jnp.asarray((kc3 >= wstart[..., None]) & (kc3 < wstart[..., None] + NA_KW))
    col_rel = np.clip(kc3 - qcol[..., None], -(NA_KW - 1), NA_KW - 1) + NA_KW - 1
    bias_cols = rpb.astype(jnp.float32)[:, :, col_rel]
    n_loc = kh * NA_KSPAN_W

    def row_block(args):
        r, r0, q_r = args
        k_rows = lax.dynamic_slice_in_dim(k_g, r0, kh, axis=1)
        v_rows = lax.dynamic_slice_in_dim(v_g, r0, kh, axis=1)
        k_blk = k_rows[:, :, kcol]
        v_blk = v_rows[:, :, kcol]
        qb = q_r.reshape(B, n_cb, NA_QBLOCK_W, H, dh)
        s_loc = jnp.einsum('bjqhd,bijlhd->bhjqil', qb, k_blk).astype(jnp.float32)
        rel_r = r0 + jnp.arange(kh) - r + NA_KH_MAX - 1
        bias = jnp.moveaxis(bias_cols[:, rel_r], 1, 3)
        s_loc = jnp.where(col_valid[:, :, None, :], s_loc + bias, NEG_INF)
        s_ctx = jnp.einsum('bjqhd,bkhd->bhjqk', qb, k_c).astype(jnp.float32)
        s = jnp.concatenate([s_loc.reshape(B, H, n_cb, NA_QBLOCK_W, n_loc), s_ctx], axis=-1)
        p = jax.nn.softmax(s, axis=-1).astype(v_g.dtype)
        p_loc = p[..., :n_loc].reshape(B, H, n_cb, NA_QBLOCK_W, kh, NA_KSPAN_W)
        p_ctx = p[..., n_loc:]
        o = (jnp.einsum('bhjqil,bijlhd->bjqhd', p_loc, v_blk)
             + jnp.einsum('bhjqk,bkhd->bjqhd', p_ctx, v_c))
        return o.reshape(B, GRID_W, H * dh)

    o = lax.map(row_block, (jnp.arange(rows), row_start, jnp.moveaxis(q_g, 1, 0)))
    y_l = jnp.moveaxis(o, 0, 1).reshape(B, S, H * dh) @ w_o
    y_c = None
    if need_ctx:
        q_cc = qc.reshape(B, -1, H, dh) * scale
        s = jnp.einsum('bqhd,bkhd->bhqk', q_cc, k_c).astype(jnp.float32)
        p = jax.nn.softmax(s, axis=-1).astype(v_c.dtype)
        oc = jnp.einsum('bhqk,bkhd->bqhd', p, v_c)
        y_c = oc.reshape(B, -1, H * dh) @ w_o
    return y_l, y_c

def setup_inputs(seed: int = 0) -> dict:
    key = jax.random.key(seed)
    ks = jax.random.split(key, 32)
    n_even = (DEPTH + 1) // 2
    n_odd = DEPTH // 2
    nrm = jax.random.normal
    D, F = D_MODEL, D_FF
    x = nrm(ks[0], (BATCH, SEQ, D), jnp.float32)
    c = nrm(ks[1], (BATCH, D), jnp.float32)
    ctx = nrm(ks[2], (BATCH, CTX_LEN, D), jnp.float32)
    c_ctx = nrm(ks[3], (D,), jnp.float32)
    w_mod = nrm(ks[4], (DEPTH, D, N_MOD * D), jnp.float32) * (0.5 * D ** -0.5)
    b_mod = nrm(ks[5], (DEPTH, N_MOD * D), jnp.float32) * 0.02
    norm_g = 1.0 + 0.02 * nrm(ks[6], (DEPTH, 3, D), jnp.float32)
    ffn_w1 = nrm(ks[7], (DEPTH, 2, D, 2 * F), jnp.float32) * D ** -0.5
    ffn_w2 = nrm(ks[8], (DEPTH, 2, F, D), jnp.float32) * F ** -0.5
    w_in_ab = nrm(ks[9], (n_even, D, AB_IN_WIDTH), jnp.float32) * D ** -0.5
    w_out_ab = nrm(ks[10], (n_even, D, D), jnp.float32) * D ** -0.5
    base_logit = jnp.log(2.0 ** (5.0 + jnp.arange(RET_HEADS, dtype=jnp.float32)) - 1.0)
    ret_decay_logit = base_logit + 0.01 * nrm(ks[11], (n_even, 2, RET_HEADS), jnp.float32)
    gp = (n_even, 2, S5_GROUPS, S5_STATE)
    s5_lam_re = -0.5 + 0.01 * nrm(ks[12], gp, jnp.float32)
    s5_lam_im = math.pi * jnp.arange(S5_STATE, dtype=jnp.float32) + 0.01 * nrm(ks[13], gp, jnp.float32)
    s5_log_dt = jax.random.uniform(ks[14], (n_even, 2, S5_GROUPS), jnp.float32,
                                   math.log(S5_DT_MIN), math.log(S5_DT_MAX))
    bsh = (n_even, 2, S5_GROUPS, S5_STATE, S5_GROUP)
    s5_b_re = nrm(ks[15], bsh, jnp.float32) * (2 * S5_GROUP) ** -0.5
    s5_b_im = nrm(ks[16], bsh, jnp.float32) * (2 * S5_GROUP) ** -0.5
    csh = (n_even, 2, S5_GROUPS, S5_GROUP, S5_STATE)
    s5_c_re = nrm(ks[17], csh, jnp.float32) * (2 * S5_STATE) ** -0.5
    s5_c_im = nrm(ks[18], csh, jnp.float32) * (2 * S5_STATE) ** -0.5
    s5_d = nrm(ks[19], (n_even, S5_WIDTH), jnp.float32)
    s5_glu_w = nrm(ks[20], (n_even, S5_WIDTH, S5_WIDTH), jnp.float32) * S5_WIDTH ** -0.5
    s5_glu_b = 0.02 * nrm(ks[21], (n_even, S5_WIDTH), jnp.float32)
    na_w_qkv = nrm(ks[22], (n_odd, D, 3 * D), jnp.float32) * D ** -0.5
    na_w_o = nrm(ks[23], (n_odd, D, D), jnp.float32) * D ** -0.5
    na_rpb = 0.02 * nrm(ks[24], (n_odd, NA_HEADS, 2 * NA_KH_MAX - 1, 2 * NA_KW - 1), jnp.float32)
    final_g = 1.0 + 0.02 * nrm(ks[25], (D,), jnp.float32)
    return {"x": x, "c": c, "ctx": ctx, "c_ctx": c_ctx, "w_mod": w_mod, "b_mod": b_mod,
            "norm_g": norm_g, "ffn_w1": ffn_w1, "ffn_w2": ffn_w2, "w_in_ab": w_in_ab,
            "w_out_ab": w_out_ab, "ret_decay_logit": ret_decay_logit, "s5_lam_re": s5_lam_re,
            "s5_lam_im": s5_lam_im, "s5_log_dt": s5_log_dt, "s5_b_re": s5_b_re, "s5_b_im": s5_b_im,
            "s5_c_re": s5_c_re, "s5_c_im": s5_c_im, "s5_d": s5_d, "s5_glu_w": s5_glu_w,
            "s5_glu_b": s5_glu_b, "na_w_qkv": na_w_qkv, "na_w_o": na_w_o, "na_rpb": na_rpb,
            "final_g": final_g}

def reference(x, c, ctx, c_ctx, w_mod, b_mod, norm_g, ffn_w1, ffn_w2, w_in_ab, w_out_ab,
              ret_decay_logit, s5_lam_re, s5_lam_im, s5_log_dt, s5_b_re, s5_b_im, s5_c_re, s5_c_im,
              s5_d, s5_glu_w, s5_glu_b, na_w_qkv, na_w_o, na_rpb, final_g):
    S = x.shape[1]
    t = jnp.arange(S)
    row = t // GRID_W
    col = t % GRID_W
    h = x
    hc = ctx
    sc = jax.nn.silu(c)
    scc = jax.nn.silu(c_ctx)
    for layer in range(DEPTH):
        last = layer == DEPTH - 1
        i = layer // 2
        ml = jnp.split((sc @ w_mod[layer] + b_mod[layer])[:, None, :], N_MOD, axis=-1)
        mc = jnp.split((scc @ w_mod[layer] + b_mod[layer])[None, None, :], N_MOD, axis=-1)
        h = h + 0.5 * ml[2] * swiglu(modulate(h, norm_g[layer, 0], ml[0], ml[1]), ffn_w1[layer, 0], ffn_w2[layer, 0])
        hc = hc + 0.5 * mc[2] * swiglu(modulate(hc, norm_g[layer, 0], mc[0], mc[1]), ffn_w1[layer, 0], ffn_w2[layer, 0])
        a_l = modulate(h, norm_g[layer, 1], ml[3], ml[4])
        a_c = modulate(hc, norm_g[layer, 1], mc[3], mc[4])
        if layer % 2 == 0:
            y_l, y_c = ab_mixer(a_l, a_c, w_in_ab[i], w_out_ab[i], ret_decay_logit[i], s5_lam_re[i],
                                s5_lam_im[i], s5_log_dt[i], s5_b_re[i], s5_b_im[i], s5_c_re[i], s5_c_im[i],
                                s5_d[i], s5_glu_w[i], s5_glu_b[i], row, col, not last)
        else:
            y_l, y_c = na_mixer(a_l, a_c, na_w_qkv[i], na_w_o[i], na_rpb[i], not last)
        h = h + ml[5] * y_l
        h = h + 0.5 * ml[8] * swiglu(modulate(h, norm_g[layer, 2], ml[6], ml[7]), ffn_w1[layer, 1], ffn_w2[layer, 1])
        if not last:
            hc = hc + mc[5] * y_c
            hc = hc + 0.5 * mc[8] * swiglu(modulate(hc, norm_g[layer, 2], mc[6], mc[7]), ffn_w1[layer, 1], ffn_w2[layer, 1])
    return rms_norm(h, final_g)


_drawn_inputs = setup_inputs


def setup_inputs(seed=0):
    import zlib

    import numpy as np

    out = dict(_drawn_inputs(seed))
    spreads = {}
    factors = {'norm_g': 6.636,
     's5_lam_re': 64.0,
     's5_lam_im': 52.712,
     's5_log_dt': 58.992,
     's5_b_re': 64.0,
     's5_b_im': 64.0,
     's5_c_re': 64.0,
     's5_c_im': 64.0,
     's5_glu_b': 32.244,
     'na_rpb': 188.625,
     'final_g': 22.93}
    for name, (base, spread) in spreads.items():
        noise = np.random.default_rng([zlib.crc32(name.encode()), seed]).standard_normal(out[name].shape)
        drawn = base * np.exp(spread * noise) if base else spread * noise
        out[name] = __import__('jax').numpy.asarray(drawn.astype(out[name].dtype))
    for name, factor in factors.items():
        out[name] = (out[name] * factor).astype(out[name].dtype)
    return out
```

```python
from contextlib import ExitStack

import numpy as np

import concourse.bass as bass
from concourse import mybir

F32 = mybir.dt.float32
F32R = mybir.dt.float32r
ALU = mybir.AluOpType
ACT = mybir.ActivationFunctionType
AX = mybir.AxisListType

P = 128
D = 1024
KT = D // P
NCTX = 256
NLAT = 256
T = NCTX + NLAT
HALVES = ((0, 0, NCTX), (1, NCTX, T))
FF = 2816
BLOCKS = (12, 10)
N_MOD = 9
GRID_W = 64
NH = 16
RELH, RELW = 15, 31
UNITS = 2 * NH
EPS = 1e-6
SUB = 512
SUBS = N_MOD * D // SUB
SUB_OPS = 2 * KT
FIRST_SUBS = 4

SEGMENTS = (
    [(f"ffn0.{s}", n) for s, n in (("up0", 12), ("down0", 8), ("up1", 10), ("down1", 8))]
    + [("s5_in", 2), ("ret_in", 8), ("glu", 2), ("ab_out", 4)]
    + [(f"ffn1.{s}", n) for s, n in (("up0", 12), ("down0", 8), ("up1", 10), ("down1", 8))]
    + [(f"ffn2.{s}", n) for s, n in (("up0", 12), ("down0", 8), ("up1", 10), ("down1", 8))]
    + [("na_q", 4), ("na_k", 4), ("na_v", 4), ("na_out", 4)]
    + [(f"ffn3.{s}", n) for s, n in (("up0", 12), ("down0", 8), ("up1", 10), ("down1", 8))]
)
BASE, SIZE, ORDER = {}, {}, []
_n = 0
for _name, _count in SEGMENTS:
    BASE[_name], SIZE[_name] = _n, _count
    ORDER.append(_name)
    _n += _count
TILES = _n

H_BASE = {}
_n = 0
for _name, _count in (("ffn0.down0", 8), ("ffn0.down1", 8), ("ab_out", 8), ("ffn1.down0", 8), ("ffn1.down1", 8),
                      ("ffn2.down0", 8), ("ffn2.down1", 8), ("na_out", 8), ("ffn3.down0", 8), ("ffn3.down1", 8)):
    H_BASE[_name] = _n
    _n += _count
H_END = _n

MOD_BESIDE = {"ffn0.up0": 4, "ffn0.down0": 10, "ffn0.up1": 14, "ffn0.down1": 19,
              "ffn1.down0": 23, "ffn1.up1": 27, "ffn1.down1": 32}

XS_D = 262
MAGIC = 1.5 * 2 ** 23
LN2_HI, LN2_LO = 0.693359375, -2.12194440e-4
TWO_PI = float(np.nextafter(np.float32(2 * np.pi), np.float32(0)))
KSCALE = float(P) ** -0.5
STATE = ("lre", "lim", "ldt", "k", "r", "t", "dt", "a", "u", "sin", "shalf", "em1", "rad", "cm1", "cos", "nre",
         "wre", "wim", "x0", "x1", "x2", "l0r", "l0i", "l1r", "l1i", "l2r", "l2i", "l3r", "l3i", "l4r", "l4i")

C_IDENT, C_SWAP, C_COS, C_SIN, C_STEP, C_WINDOW = 0, 128, 256, 512, 768, 1024
C_END = 1088


def shape_constants():
    c = np.zeros((P, C_END), np.float32)
    c[:, C_IDENT:C_IDENT + P] = np.eye(P)
    partner = np.arange(P) ^ 32
    c[partner, C_SWAP + np.arange(P)] = 1.0
    t = np.arange(NLAT)
    inv = (np.float32(10000.0) ** (-np.arange(0, 64, 2, dtype=np.float32) / np.float32(64))).astype(np.float32)
    for p in range(P):
        pos = (t // GRID_W if p < 64 else t % GRID_W).astype(np.float32)
        ang = (pos * inv[p % 32]).astype(np.float32)
        c[p, C_COS:C_COS + NLAT] = np.cos(ang)
        c[p, C_SIN:C_SIN + NLAT] = np.sin(ang) * (-1.0 if (p // 32) % 2 == 0 else 1.0)
    c[:, C_STEP:C_STEP + 2 * P] = np.concatenate(
        [np.arange(1, P + 1), np.arange(64, 0, -1), np.arange(P, 64, -1)])
    q = GRID_W - 1 - np.arange(P)[:, None] % GRID_W
    k = np.arange(GRID_W)[None, :]
    start = np.clip(q - 8, 0, GRID_W - 16)
    c[:, C_WINDOW:C_WINDOW + GRID_W] = np.where((k >= start) & (k < start + 16), 3e38, -1e30)
    return c


def shape_lags():
    j = (np.arange(2)[None, :, None] * P + np.arange(P)[:, None, None]).astype(np.float32)
    i = np.arange(256, dtype=np.float32)[None, None, :]
    d = i - j
    out = np.stack([np.maximum(d, 0), (d >= 0) * 1.0, np.maximum(-d, 0), (d <= 0) * 1.0, 256 + d, 256 - d], 1)
    return np.ascontiguousarray(out.reshape(P, 6 * 512).astype(np.float32))


def program(nc, i, out):
    with ExitStack() as ctx:
        def sem(name):
            return ctx.enter_context(nc.semaphore(name))

        def sbuf(name, shape, dt=F32, scope=ctx):
            return scope.enter_context(nc.sbuf_tensor(name, shape, dt))

        const = sbuf("const", [P, C_END])
        ones = sbuf("ones", [P, P])
        eps = sbuf("eps", [P, 1])
        h = sbuf("h", [P, KT, T])
        a_hi = sbuf("a_hi", [P, KT, T], F32R)
        a_lo = sbuf("a_lo", [P, KT, T], F32R)
        w_raw = sbuf("w_raw", [P, 2, 2048])
        w_hi = sbuf("w_hi", [P, 2, 2048], F32R)
        w_lo = sbuf("w_lo", [P, 2, 2048], F32R)
        bias_mod = sbuf("bias_mod", [P, 2 * N_MOD * KT])
        gains = sbuf("gains", [P, 56])
        cond = sbuf("cond", [P, KT, 2])
        glu_b = sbuf("glu_b", [P, 4])
        half_pi = sbuf("half_pi", [P, 1])
        rows_t = sbuf("rows_t", [P, 16])
        modv = sbuf("modv", [P, 2 * N_MOD * KT, 2])
        gain = sbuf("gain", [P, 2, KT])
        sq = sbuf("sq", [P, 2, T])
        std = sbuf("std", [P, T])
        rstd = sbuf("rstd", [P, T])
        scaled = sbuf("scaled", [P, 2, T])
        normed = sbuf("normed", [P, 2, T])
        gate = sbuf("gate", [P, 2, KT])

        ps = [ctx.enter_context(nc.psum_tensor(f"ps{n}", [P, 2, 512], F32)) for n in range(2)]
        bank = [ctx.enter_context(nc.psum_tensor(f"bank{n}", [P, 512], F32)) for n in range(4)]
        ps_mod, ps_sum = bank[2], bank[3]

        with ExitStack() as ffn:
            g_hi = sbuf("g_hi", [P, BLOCKS[0], T], F32R, ffn)
            g_lo = sbuf("g_lo", [P, BLOCKS[0], T], F32R, ffn)
            sil = sbuf("sil", [P, 2, T], F32, ffn)
            gated = sbuf("gated", [P, 2, T], F32, ffn)
            with ExitStack() as mod:
                mod_raw = sbuf("mod_raw", [P, 2, KT // 2, SUB], F32, mod)
                mod_acc = sbuf("mod_acc", [P, 2, SUB], F32, mod)
            bias = sbuf("bias", [P, NH, 6, GRID_W], F32, ffn)
        with ExitStack() as start:
            tokens = sbuf("tokens", [P, 4, D], F32, start)
            rows = sbuf("rows", [P, 2, P], F32, start)

        with ExitStack() as end:
            out_rows = sbuf("out_rows", [P, 2, D], F32, end)
        with ExitStack() as s5:
            tcos = sbuf("tcos", [P, 2, 16, P], F32, s5)
            tsin = sbuf("tsin", [P, 2, 16, P], F32, s5)
            us = sbuf("us", [P, 16, P], F32, s5)
            b_in = sbuf("b_in", [P, 2, 2, 16, 16], F32, s5)
            c_in = sbuf("c_in", [P, 2, 2, 16, 16], F32, s5)
            pows = sbuf("pows", [P, 2, 2, 16, 5], F32, s5)
            wpows = sbuf("wpows", [P, 2, 2, 16, 4], F32, s5)
            r4 = sbuf("r4", [P, 2, 16], F32, s5)
            skip = sbuf("skip", [P, 16], F32, s5)
            with ExitStack() as prep:
                b_raw = sbuf("b_raw", [P, 2, 2, 16, 16], F32, prep)
                crow = sbuf("crow", [P, 2, 2, 4, 2, 64], F32, prep)
                prow = sbuf("prow", [32, 3, P], F32, prep)
                dtrow = sbuf("dtrow", [32, 2], F32, prep)
                drow = sbuf("drow", [16, 2, P], F32, prep)
                pt = sbuf("pt", [P, 32, 32], F32, prep)
                kint = sbuf("kint", [P, 32], mybir.dt.int32, prep)
                bt = sbuf("bt", [P, 4, 512], F32, prep)
            cp = sbuf("cp", [P, 2, 2, 16, 32], F32, s5)
            wb = sbuf("wb", [P, 2, 2, 2, 4, 32], F32, s5)
            vt = sbuf("vt", [P, 2, 4, P], F32, s5)
            kt = sbuf("kt", [P, 2, P], F32, s5)
            prod = sbuf("prod", [P, 4, 128], F32, s5)
            cprod = sbuf("cprod", [P, 4, 160], F32, s5)
            rot = sbuf("rot", [P, 2, 2, 2, P], F32, s5)
            zs = sbuf("zs", [P, 2, 2, P], F32, s5)
            back = sbuf("back", [P, 2, 2, 2, P], F32, s5)
            xs = sbuf("xs", [P, 2, 2 * XS_D], F32, s5)
        with ExitStack() as ret:
            y = sbuf("y", [P, 4, T], F32, ret)
            qk = sbuf("qk", [P, 8, T], F32, ret)
            vtok = sbuf("vtok", [P, 4, 512], F32, ret)
            gs = sbuf("gs", [P, 4, T], F32, ret)
            lags = sbuf("lags", [P, 6, 512], F32, ret)
            lgam = sbuf("lgam", [P, 8], F32, ret)
            lg = sbuf("lg", [P, 4, 8], F32, ret)
            ex = sbuf("ex", [P, 4, 512], F32, ret)
            decay = sbuf("decay", [P, 2, T], F32, ret)
            scores = sbuf("scores", [P, 4, T], F32, ret)
        with ExitStack() as na:
            q_t = sbuf("q_t", [P, KT, NLAT], F32, na)
            k_t = sbuf("k_t", [P, KT, T], F32, na)
            v_tok = sbuf("v_tok", [P, 4, D], F32, na)
            prob = sbuf("prob", [P, 2, T], F32, na)
            prob_t = sbuf("prob_t", [P, 2, T], F32, na)
            diag = sbuf("diag", [P, 2, P], F32, na)
            negmax = sbuf("negmax", [P, UNITS], F32, na)
            rowsum = sbuf("rowsum", [P, UNITS], F32, na)
            recip = sbuf("recip", [P, UNITS], F32, na)
        const_in, rows_in, tokens_in = sem("const_in"), sem("rows_in"), sem("tokens_in")
        set_done = sem("set_done")
        rows_turned, rows_copied = sem("rows_turned"), sem("rows_copied")
        cond_ready = sem("cond_ready")
        token_turned, token_copied = sem("token_turned"), sem("token_copied")
        w_in = [sem("w_in0"), sem("w_in1")]
        hi_ready, lo_ready = sem("hi_ready"), sem("lo_ready")
        pe_done = sem("pe_done")
        ps_free = [sem("ps_free0"), sem("ps_free1")]
        mod_in = [sem("mod_in0"), sem("mod_in1")]
        mod_step, mod_summed, mod_ready = sem("mod_step"), sem("mod_summed"), sem("mod_ready")
        sil_ready, g_split = sem("sil_ready"), sem("g_split")
        sq_ready, sq_summed = sem("sq_ready"), sem("sq_summed")
        std_ready, rstd_ready, scaled_ready = sem("std_ready"), sem("rstd_ready"), sem("scaled_ready")
        normed_ready, a_ready, gain_ready = sem("normed_ready"), sem("a_ready"), sem("gain_ready")
        pool_hi = sem("pool_hi")
        dve_chain = sem("dve_chain")
        final_ready = sem("final_ready")
        s5_sem = {n: sem("s5_" + n) for n in (
            "rows", "bias", "pads", "loads", "spread", "turned_rows", "c_turned", "c_copied", "c_done", "act", "tanh",
            "sin", "tables", "us_act", "wprod", "w", "cprod", "cre", "cprod_im", "cim", "turned", "kmm", "vt", "k", "v",
            "rot", "z", "half", "scan", "back", "x", "y", "gelu", "ready")}
        ret_sem = {n: sem("ret_" + n) for n in (
            "loads", "evac", "swapped", "rope", "exp1", "exp2", "gam", "mask", "s", "p", "o", "osq", "sum", "std",
            "y_split", "done", "sig", "glu", "mix")}
        na_sem = {n: sem("na_" + n) for n in (
            "bias", "masked", "s", "added", "max", "exp", "recip", "diag", "turned", "copied", "o",
            "hi", "mix")}
        out_turned, out_copied, out_stored = sem("out_turned"), sem("out_copied"), sem("out_stored")

        NORM_OF = (0, 2, 3, 5)
        FFN_T0 = (0, 0, 0, NCTX)
        NORM_T0 = (0, 0, 0, 0, 0, NCTX, NCTX)

        def width(segment):
            if "down" in segment:
                return BLOCKS[int(segment[-1])] * P
            return 4 * 256 if segment == "glu" else 2048

        def g_base(segment):
            return 22 * int(segment[3]) + (BLOCKS[0] if segment.endswith("1") else 0)

        def segment_of(n):
            for s in ORDER:
                if BASE[s] <= n < BASE[s] + SIZE[s]:
                    return s
            return None

        def halves(t0):
            return [x for x in HALVES if x[1] >= t0]

        def col(norm, which):
            return (norm // 3) * N_MOD * KT + (3 * (norm % 3) + which) * KT

        def last_h_tile(norm):
            return {1: "ffn0.down1", 2: "ab_out", 3: "ffn1.down1", 4: "ffn2.down1", 5: "na_out", 6: "ffn3.down1"}[norm]

        block = ctx.enter_context(nc.Block())

        def early(value, n):
            return isinstance(value, int) and value < n

        def unit(it, x):
            it, x = it + x // 8, x % 8
            return it, x, 8 * it + x, x % 2, 4 * it + x // 2, 2 * it + x // 4

        def attention(engine, prologue, step):
            prologue()
            if engine is nc.tensor:
                for u in range(UNITS):
                    step(u // 8, u % 8, u < UNITS - 2)
                return
            for x in range(8):
                step(0, x, True)
            with engine.Fori(1, UNITS // 8 - 1) as it:
                for x in range(8):
                    step(it, x, True)
            for x in range(8):
                step(UNITS // 8 - 1, x, x < 6)

        def q_(name):
            return pt[:, STATE.index(name), :]

        def c_products(engine, pair, which):
            for n in which:
                x, z = ((0, 0), (1, 1), (0, 1), (1, 0))[n]
                c = c_in[:, x, :, bass.ds(pair, 1), :].broadcast_to([P, 2, 5, 16])
                l = pows[:, z, :, bass.ds(pair, 1), :].rearrange("p d a n -> p d n a").broadcast_to([P, 2, 5, 16])
                ins = engine.tensor_tensor(cprod[:, n, :].rearrange("p (d n k) -> p d n k", d=2, n=5), c, l, ALU.mult)
            return ins

        def c_combine(engine, pair, slot, ri, op):
            for g in range(2):
                at = slice(64 * g, 64 * g + 64)
                ins = engine.tensor_tensor(cp[at, slot, ri, 3:13, 16 * g:16 * g + 16],
                                           cprod[at, 2 * ri, :].rearrange("p (n k) -> p n k", k=16),
                                           cprod[at, 2 * ri + 1, :].rearrange("p (n k) -> p n k", k=16), op)
            return ins

        def mixer_loads(sp, segment):
            if segment == "ret_in":
                sp.wait_ge(pe_done, BASE["s5_in"])
                sp.wait_ge(mod_ready, 23)
                for n, x in enumerate(("s5_lam_re", "s5_lam_im")):
                    sp.dma_start(prow[:, n, :], i[x][0].rearrange("d (q g) s -> (d q) (g s)", g=2)).then_inc(s5_sem["rows"], 16)
                sp.dma_start(dtrow[:], i["s5_log_dt"][0].rearrange("d (q g) -> (d q) g", g=2)).then_inc(s5_sem["rows"], 16)
                sp.dma_start(drow[:, 0, 0:32], i["s5_d"][0].rearrange("(q c) -> q c", c=32)).then_inc(s5_sem["rows"], 16)
                for n, x in enumerate(("s5_c_re", "s5_c_im")):
                    for dup in range(2):
                        sp.dma_start(crow[:, n, :, :, dup, :].rearrange("p d q s -> p (d q) s"),
                                     i[x][0].rearrange("d (q a) k s -> (a k) (d q) s", a=8)).then_inc(s5_sem["loads"], 16)
                for n, x in enumerate(("s5_b_re", "s5_b_im")):
                    for d in range(2):
                        src = i[x][0, d].rearrange("(q g) s k -> g s q k", g=2)
                        for g in range(2):
                            sp.dma_start(b_raw[64 * g:64 * g + 64, n, d], src[g]).then_inc(s5_sem["loads"], 16)
            if segment == "ffn2.down0":
                sp.wait_ge(mod_ready, 2 * SUBS)
                for hd in range(NH):
                    for b in range(2):
                        src = bass.AP(tensor=i["na_rpb"].tensor, offset=hd * RELH * RELW + (5 - b) * RELW - 48,
                                      ap=[[1, GRID_W], [RELW, 6], [1, GRID_W]])
                        sp.dma_start(bias[64 * b:64 * b + 64, hd], src).then_inc(na_sem["bias"], 16)
            if segment == "glu":
                sp.wait_ge(s5_sem["y"], 16)
                sp.dma_start(lags[:].rearrange("p a b -> p (a b)"), i["lags"]).then_inc(ret_sem["loads"], 16)
                sp.dma_start(lgam[:], i["ret_decay_logit"][0].rearrange("(a d) h -> a (d h)", a=1).broadcast_to([P, 8])
                             ).then_inc(ret_sem["loads"], 16)

        @block.sync
        def _(sp):
            sp.dma_start(const[:], i["const"]).then_inc(const_in, 16)
            sp.dma_start(rows[0:72, 0, :], i["b_mod"][0].rearrange("(r c) -> r c", c=P)).then_inc(rows_in, 16)
            sp.dma_start(rows[72:120, 0, :], i["norm_g"].rearrange("l n (r c) -> (l n r) c", c=P)).then_inc(rows_in, 16)
            sp.dma_start(rows[120:128, 0, :], i["final_g"].rearrange("(r c) -> r c", c=P)).then_inc(rows_in, 16)
            sp.dma_start(rows[0:72, 1, :], i["b_mod"][1].rearrange("(r c) -> r c", c=P)).then_inc(rows_in, 16)
            sp.dma_start(rows[72:80, 1, :], i["c_ctx"].rearrange("(r c) -> r c", c=P)).then_inc(rows_in, 16)
            sp.dma_start(rows[80:88, 1, :], i["c"][0].rearrange("(r c) -> r c", c=P)).then_inc(rows_in, 16)
            sp.dma_start(rows[88:92, 1, :], i["s5_glu_b"][0].rearrange("(r c) -> r c", c=P)).then_inc(rows_in, 16)

            def fetch_mod(s, layer):
                w = i["w_mod"][layer].rearrange("(k p) n -> p k n", p=P)
                cols = bass.ds((s - layer * SUBS) * SUB, SUB)
                for half in range(2):
                    def one(half=half):
                        sp.dma_start(mod_raw[:, half], w[:, 4 * half:4 * half + 4, cols]).then_inc(mod_in[half], 16)
                    yield half, one

            def fetch_mod_after(s, layer, half, one):
                sp.wait_ge(mod_step, SUB_OPS * (s - 1) + 8 * (half + 1))
                one()

            def fetch_weights(segment, j, slot, free):
                dst = w_raw[:, slot]
                if free is not None:
                    sp.wait_ge(lo_ready, free)
                if "up" in segment:
                    f, b = int(segment[3]), int(segment[-1])
                    w = i["ffn_w1"][f // 2, f % 2].rearrange("(k p) (h f) -> p k h f", p=P, h=2)
                    at = bass.ds((j + (BLOCKS[0] if b else 0)) * P, P)
                    d = dst.rearrange("p (k h f) -> p k h f", k=KT, h=2)
                    parts = [(d[:, :, x], w[:, :, x, at]) for x in range(2)]
                elif "down" in segment:
                    f, b = int(segment[3]), int(segment[-1])
                    k0, n = (BLOCKS[0] if b else 0), BLOCKS[b]
                    w = i["ffn_w2"][f // 2, f % 2].rearrange("(k p) d -> p k d", p=P)
                    at = bass.ds(j * P, P)
                    d = dst[:, 0:n * P].rearrange("p (k f) -> p k f", k=n)
                    parts = [(d[:, x:x + n // 2], w[:, k0 + x:k0 + x + n // 2, at]) for x in (0, n // 2)]
                else:
                    src, c0, n = {"s5_in": ("w_in_ab", 2048, 8), "ret_in": ("w_in_ab", 0, 8), "glu": ("s5_glu_w", 0, 4),
                                  "ab_out": ("w_out_ab", 0, 8), "na_q": ("na_w_qkv", 0, 8), "na_k": ("na_w_qkv", D, 8),
                                  "na_v": ("na_w_qkv", 2 * D, 8), "na_out": ("na_w_o", 0, 8)}[segment]
                    w = i[src][0].rearrange("(k p) n -> p k n", p=P)
                    at = bass.ds(j * 256 + c0, 256)
                    d = dst[:, 0:n * 256].rearrange("p (k f) -> p k f", k=n)
                    parts = [(d[:, x:x + n // 2], w[:, x:x + n // 2, at]) for x in (0, n // 2)]
                for d, s in parts:
                    sp.dma_start(d, s).then_inc(w_in[slot], 16)

            def body(segment, it, first=False, mod_at=None):
                piece = []
                if mod_at is not None:
                    s = it + MOD_BESIDE[segment]
                    layer = 1 if (s >= SUBS if isinstance(s, int) else MOD_BESIDE[segment] >= SUBS) else 0
                    piece = list(fetch_mod(s, layer))
                for slot in range(2):
                    fetch_weights(segment, 2 * it + slot, slot,
                                  None if first else BASE[segment] + 2 * it + slot - 1)
                    if piece:
                        fetch_mod_after(s, layer, *piece[slot])

            for s in range(FIRST_SUBS):
                for half, one in fetch_mod(s, 0):
                    if s:
                        fetch_mod_after(s, 0, half, one)
                    else:
                        one()
                if s == 0:
                    x = i["ctx"][0].rearrange("(t p) d -> p t d", p=P)
                    y = i["x"][0].rearrange("(t p) d -> p t d", p=P)
                    sp.dma_start(tokens[:, 0:2], x).then_inc(tokens_in, 16)
                    sp.dma_start(tokens[:, 2:4], y).then_inc(tokens_in, 16)
            for segment in ORDER:
                mixer_loads(sp, segment)
                its = SIZE[segment] // 2
                mod = segment if segment in MOD_BESIDE else None
                first = segment == ORDER[0]
                lo, hi = 0, its
                if first:
                    body(segment, 0, True, mod)
                    lo = 1
                if segment == "ffn0.up1":
                    hi = its - 1
                if hi - lo > 1:
                    with sp.Fori(lo, hi) as it:
                        body(segment, it, False, mod)
                    lo = hi
                for it in range(lo, its):
                    body(segment, it, False, mod)
            sp.wait_ge(out_copied, KT)
            for t in range(2):
                sp.dma_start(out[0, t * P:(t + 1) * P, :], out_rows[:, t, :]).then_inc(out_stored, 16)
            sp.wait_ge(out_stored, 32)

        @block.scalar
        def _(act):
            def split_hi(n, size, slot):
                act.wait_ge(w_in[slot], 16 * (n + 2 - slot))
                if not early(n, 2):
                    act.wait_ge(pe_done, n - 1)
                nc.scalar.activation(w_hi[:, slot, 0:size], w_raw[:, slot, 0:size], ACT.Copy).then_inc(hi_ready, 1)

            def up(segment):
                t0 = FFN_T0[int(segment[3])]

                def body(it, last):
                    for slot in range(2):
                        n = BASE[segment] + 2 * it + slot
                        nxt = width(segment) if not (last and slot) else width(segment_of(BASE[segment] + SIZE[segment]))
                        split_hi(n + 1, nxt, 1 - slot)
                        act.wait_ge(pe_done, n + 1)
                        nc.scalar.activation(sil[:, slot, t0:T], ps[slot][:, 0, t0:T], ACT.Silu).then_inc(sil_ready, 1)

                first = 1 if BASE[segment] == 0 else 0
                if first:
                    body(0, False)
                with act.Fori(first, SIZE[segment] // 2 - 1) as it:
                    body(it, False)
                body(SIZE[segment] // 2 - 1, True)

            def down(segment):
                nxt = segment_of(BASE[segment] + SIZE[segment])
                if SIZE[segment] > 2:
                    with act.Fori(0, SIZE[segment] // 2 - 1) as it:
                        for slot in range(2):
                            split_hi(BASE[segment] + 2 * it + slot + 1, width(segment), 1 - slot)
                n = BASE[segment] + SIZE[segment] - 2
                split_hi(n + 1, width(segment), 1)
                if nxt:
                    split_hi(n + 2, width(nxt), 0)

            def norm(k_norm):
                t0 = NORM_T0[k_norm]
                for k in range(KT):
                    if k_norm:
                        n = BASE[last_h_tile(k_norm)] + (k if "down" in last_h_tile(k_norm) else k // 2)
                        act.wait_ge(ps_free[n % 2], n // 2 + 1)
                    else:
                        act.wait_ge(token_copied, k + 1)
                    if KT * k_norm + k >= 2:
                        act.wait_ge(sq_summed, KT * k_norm + k - 1)
                    nc.scalar.activation(sq[:, k % 2, t0:T], h[:, k, t0:T], ACT.Square).then_inc(sq_ready, 1)
                act.wait_ge(sq_summed, KT * (k_norm + 1))
                nc.scalar.activation(std[:, t0:T], ps_sum[:, t0:T], ACT.Sqrt, bias=eps[:, 0:1],
                                     scale=1.0 / D).then_inc(std_ready, 1)
                if k_norm == 6:
                    return
                act.wait_ge(gain_ready, k_norm + 1)
                for k in range(KT):
                    act.wait_ge(scaled_ready, KT * k_norm + k + 1)
                    if KT * k_norm + k >= 2:
                        act.wait_ge(a_ready, KT * k_norm + k - 1)
                    for half, b, e in halves(t0):
                        ins = nc.scalar.activation(normed[:, k % 2, b:e], scaled[:, k % 2, b:e], ACT.Identity,
                                                   bias=modv[:, col(k_norm, 0) + k, half:half + 1],
                                                   scale=gain[:, half, k:k + 1])
                    ins.then_inc(normed_ready, 1)

            def mixer0():
                S, R = s5_sem, ret_sem
                norm(1)
                for j in range(2):
                    split_hi(BASE["s5_in"] + j + 1, 2048, 1 - j)
                    act.wait_ge(pe_done, BASE["s5_in"] + j + 1)
                    for q in range(0, 2):
                        for s in range(4):
                            ins = nc.scalar.activation(
                                us[32 * s:32 * s + 32, 8 * j + q:8 * j + q + 5:4, :],
                                ps[j][32 * q:32 * q + 32, :, s::4], ACT.Copy)
                    ins.then_inc(S["us_act"], 1)
                act.wait_ge(S["act"], 1)
                nc.scalar.activation(q_("t"), q_("r"), ACT.Tanh, scale=0.5).then_inc(S["tanh"], 1)
                act.wait_ge(S["act"], 2)
                nc.scalar.activation(q_("t"), q_("a"), ACT.Tanh, scale=0.5).then_inc(S["tanh"], 1)
                nc.scalar.activation(q_("sin"), q_("u"), ACT.Sin, scale=TWO_PI).then_inc(S["sin"], 1)
                nc.scalar.activation(q_("shalf"), q_("u"), ACT.Sin, scale=TWO_PI / 2).then_inc(S["sin"], 1)
                for ri in range(2):
                    for d in range(2):
                        act.wait_ge(S["c_turned"], 2 * ri + d + 1)
                        src = bank[d][:].rearrange("p (q g k) -> p q g k", q=16, g=2)
                        for g in range(2):
                            ins = nc.scalar.activation(c_in[64 * g:64 * g + 64, ri, d], src[64 * g:64 * g + 64, :, g, :],
                                                       ACT.Copy)
                        ins.then_inc(S["c_copied"], 1)
                act.wait_ge(S["act"], 3)
                nc.scalar.activation(tsin[:], tsin[:], ACT.Sin, scale=TWO_PI).then_inc(S["tables"], 1)
                nc.scalar.activation(tcos[:], tcos[:], ACT.Sin, bias=half_pi[:, 0:1], scale=-TWO_PI).then_inc(S["tables"], 1)

                def turned(pair, slot):
                    act.wait_ge(S["turned"], pair + 1)
                    nc.scalar.activation(vt[:, slot].rearrange("p a b -> p (a b)"), bank[0][:], ACT.Copy).then_inc(S["vt"], 1)

                turned(0, 0)
                with act.Fori(0, 3) as it:
                    for q in range(4):
                        turned(4 * it + q + 1, (q + 1) % 2)
                for q in range(3):
                    turned(12 + q + 1, (q + 1) % 2)
                act.wait_ge(S["y"], 16)
                for q in range(4):
                    for t in range(4):
                        ins = nc.scalar.activation(
                            y[32 * q:32 * q + 32, :, t::4],
                            ps[q // 2][32 * t:32 * t + 32, q % 2, :].rearrange("p (m j) -> p m j", m=4),
                            ACT.Gelu_apprx_tanh)
                    ins.then_inc(S["gelu"], 1)
                base = BASE["ret_in"]
                for j in range(8):
                    n = base + j
                    split_hi(n + 1, 2048 if j < 7 else width("glu"), 1 - j % 2)
                    act.wait_ge(pe_done, n + 1)
                    p = ps[j % 2]
                    if j < 4:
                        for m in range(2):
                            ins = nc.scalar.activation(qk[:, 2 * j + m, :], p[:, m, :], ACT.Copy)
                        ins.then_inc(ps_free[j % 2], 1)
                    elif j < 6:
                        nc.scalar.activation(vtok[:, :, (j - 4) * 256:(j - 3) * 256],
                                             p[:].rearrange("p a (b c) -> p (a b) c", b=2), ACT.Copy).then_inc(ps_free[j % 2], 1)
                    else:
                        for m in range(2):
                            ins = nc.scalar.activation(gs[:, 2 * (j - 6) + m, :], p[:, m, :], ACT.Silu)
                        ins.then_inc(ps_free[j % 2], 1)
                act.wait_ge(R["gam"], 1)
                nc.scalar.activation(lg[:, 1, :], lg[:, 0, :], ACT.Exp, scale=-1.0).then_inc(R["exp1"], 1)
                act.wait_ge(R["exp1"], 1)
                nc.scalar.activation(lg[:, 2, :], lg[:, 1, :], ACT.Ln, bias=ones[:, 0:1]).then_inc(R["exp1"], 1)
                act.wait_ge(R["gam"], 2)
                for hd in range(4):
                    if hd:
                        act.wait_ge(R["mask"], hd)
                    for n, d in enumerate((0, 1, 0, 1)):
                        src = lags[:, (0, 2, 4, 5)[n], :]
                        ins = nc.scalar.activation(ex[:, n, :], src, ACT.Exp, scale=lg[:, 3, 4 * d + hd:4 * d + hd + 1])
                    ins.then_inc(R["exp2"], 1)
                    act.wait_ge(R["o"], hd + 1)
                    if hd:
                        act.wait_ge(R["sum"], hd)
                    nc.scalar.activation(sq[:, 0, :], ps_sum[:], ACT.Square).then_inc(R["osq"], 1)
                    act.wait_ge(R["sum"], hd + 1)
                    if hd:
                        act.wait_ge(R["mix"], hd)
                    nc.scalar.activation(std[:], bank[0][:], ACT.Sqrt, bias=eps[:, 0:1], scale=1.0 / P).then_inc(R["std"], 1)
                act.wait_ge(R["mix"], 4)
                for j in range(2):
                    n = BASE["glu"] + j
                    split_hi(n + 1, width("glu") if j == 0 else 2048, 1 - j)
                    act.wait_ge(pe_done, n + 1)
                    for m in range(2):
                        ins = nc.scalar.activation(gs[:, 2 * j + m, :], ps[j][:, m, :], ACT.Sigmoid,
                                                   bias=glu_b[:, 2 * j + m:2 * j + m + 1])
                    ins.then_inc(ps_free[j], 1)
                down("ab_out")

            def mixer1():
                N = na_sem
                norm(4)
                for segment in ("na_q", "na_k", "na_v"):
                    for j in range(4):
                        n = BASE[segment] + j
                        split_hi(n + 1, 2048, 1 - j % 2)
                        act.wait_ge(pe_done, n + 1)
                        p = ps[j % 2]
                        for m in range(2):
                            if segment == "na_q":
                                ins = nc.scalar.activation(
                                    q_t[:, 2 * j + m, :].rearrange("p (r c) -> p r c", c=GRID_W),
                                    p[:, m, NCTX:T].rearrange("p (r c) -> p r c", c=GRID_W)[:, :, ::-1],
                                    ACT.Copy, scale=0.125)
                            elif segment == "na_k":
                                ins = nc.scalar.activation(k_t[:, 2 * j + m, :], p[:, m, :], ACT.Copy)
                        if segment == "na_v":
                            ins = nc.scalar.activation(v_tok[:, :, j * 256:(j + 1) * 256],
                                                       p[:].rearrange("p a (b c) -> p (a b) c", b=2), ACT.Copy)
                        ins.then_inc(ps_free[j % 2], 1)

                def exps(it, x):
                    it, x, u, s, _, _ = unit(it, x)
                    act.wait_ge(N["max"], u + 1)
                    if not early(u, 2):
                        act.wait_ge(N["turned"], u - 1)
                    nc.scalar.activation(prob[:, s, :], ps[0][:, s, :], ACT.Exp, bias=negmax[:, bass.ds(u, 1)],
                                         accum_out=rowsum[:, bass.ds(u, 1)]).then_inc(N["exp"], 1)

                def step(it, x, more):
                    _, _, u, s, _, tile = unit(it, x)
                    act.wait_ge(N["turned"], u + 1)
                    if not early(u, 2):
                        act.wait_ge(N["o"], u - 1)
                    nc.scalar.activation(prob_t[:, s, :], ps[1][:, s, :], ACT.Copy).then_inc(N["copied"], 1)
                    if more:
                        exps(it, x + 2)
                    if x % 4 == 3:
                        act.wait_ge(N["o"], u + 1)
                        nc.scalar.activation(
                            a_hi[:, bass.ds(tile, 1), NCTX:T].rearrange("p a (r c) -> p (a r) c", c=GRID_W),
                            bank[x // 4][:, 0:NLAT].rearrange("p (r c) -> p r c", c=GRID_W)[:, :, ::-1],
                            ACT.Copy).then_inc(N["hi"], 1)

                def prologue():
                    exps(0, 0)
                    exps(0, 1)

                attention(act, prologue, step)
                down("na_out")

            act.wait_ge(rows_copied, 2)
            nc.scalar.activation(cond[:, :, 0], rows_t[:, 0:KT], ACT.Silu).then_inc(cond_ready, 1)
            nc.scalar.activation(cond[:, :, 1], rows_t[:, KT:2 * KT], ACT.Silu).then_inc(cond_ready, 1)
            for k in range(KT):
                act.wait_ge(token_turned, k + 1)
                nc.scalar.activation(h[:, k, :], bank[k % 2][:, :], ACT.Copy).then_inc(token_copied, 1)
            act.wait_ge(set_done, 1)
            act.wait_ge(w_in[0], 32)
            nc.scalar.activation(w_hi[:, 0, :], w_raw[:, 0, :], ACT.Copy).then_inc(hi_ready, 1)
            for f in range(4):
                if f == 1:
                    mixer0()
                if f == 3:
                    mixer1()
                norm(NORM_OF[f])
                for b in range(2):
                    up(f"ffn{f}.up{b}")
                    down(f"ffn{f}.down{b}")
            norm(6)
            for k in range(KT):
                act.wait_ge(out_turned, k + 1)
                nc.scalar.activation(out_rows[:, :, k * P:(k + 1) * P],
                                     bank[k % 2][:, 0:256].rearrange("p (t f) -> p t f", t=2),
                                     ACT.Copy).then_inc(out_copied, 1)

        @block.vector
        def _(dve):
            chain = [0]

            def link(ins):
                chain[0] += 1
                ins.then_inc(dve_chain, 1)
                dve.wait_ge(dve_chain, chain[0])

            def split_lo(n, size, slot):
                dve.wait_ge(hi_ready, n + 1)
                nc.vector.tensor_tensor(w_lo[:, slot, 0:size], w_raw[:, slot, 0:size],
                                        w_hi[:, slot, 0:size].bitcast(F32), ALU.subtract).then_inc(lo_ready, 1)

            def mod_half(s, half):
                dve.wait_ge(mod_in[half], 16 * (s + 1))
                for k in range(4 * half, 4 * half + 4):
                    for v in range(2):
                        src, c = mod_raw[:, half, k % 4, :], cond[:, k, v:v + 1]
                        if k == 0:
                            ins = nc.vector.tensor_scalar(mod_acc[:, v, :], src, c, None, ALU.mult)
                        else:
                            dve.wait_ge(mod_step, SUB_OPS * s + 2 * k + v - 1)
                            ins = nc.vector.scalar_tensor_tensor(mod_acc[:, v, :], src, c, mod_acc[:, v, :],
                                                                 ALU.mult, ALU.add)
                        ins.then_inc(mod_step, 1)

            def mod_collect(s):
                dve.wait_ge(mod_summed, s + 1)
                at = bass.ds(4 * s, 4)
                nc.vector.tensor_tensor(modv[:, at, :], ps_mod[:, 0:8].rearrange("p (m v) -> p m v", v=2),
                                        bias_mod[:, at].rearrange("p (m a) -> p m a", a=1).broadcast_to([P, 4, 2]),
                                        ALU.add).then_inc(mod_ready, 1)

            def up(segment):
                t0 = FFN_T0[int(segment[3])]

                def body(it, last):
                    for slot in range(2):
                        n = BASE[segment] + 2 * it + slot
                        nxt = width(segment) if not (last and slot) else width(segment_of(BASE[segment] + SIZE[segment]))
                        split_lo(n + 1, nxt, 1 - slot)
                        if segment in MOD_BESIDE:
                            mod_half(MOD_BESIDE[segment] + it, slot)
                        dve.wait_ge(sil_ready, g_base(segment) + 2 * it + slot + 1)
                        dve.wait_ge(g_split, g_base(segment) + 2 * it + slot + 1)
                        nc.vector.tensor_tensor(gated[:, slot, t0:T], sil[:, slot, t0:T], ps[slot][:, 1, t0:T],
                                                ALU.mult).then_inc(ps_free[slot], 1)
                    if segment in MOD_BESIDE:
                        mod_collect(MOD_BESIDE[segment] + it)

                with dve.Fori(0, SIZE[segment] // 2 - 1) as it:
                    body(it, False)
                body(SIZE[segment] // 2 - 1, True)

            def residual(n, slot, at, pair, t0, gated_by=gate):
                dve.wait_ge(pe_done, n + 1)
                for m in range(pair):
                    for half, b, e in halves(t0):
                        ins = nc.vector.scalar_tensor_tensor(
                            h[:, bass.ds(at + m, 1), b:e].rearrange("p a t -> p (a t)"),
                            ps[slot][:, m, b:e], gated_by[:, half, bass.ds(at + m, 1)],
                            h[:, bass.ds(at + m, 1), b:e].rearrange("p a t -> p (a t)"), ALU.mult, ALU.add)
                ins.then_inc(ps_free[slot], 1)

            def down(segment):
                f, b = int(segment[3]), int(segment[-1])
                if b == 0:
                    dve.wait_ge(mod_ready, (col(NORM_OF[f], 2) + KT) // 4)
                    for v in range(2):
                        ins = nc.vector.tensor_scalar(gate[:, v, :], modv[:, col(NORM_OF[f], 2):col(NORM_OF[f], 2) + KT, v],
                                                      0.5, None, ALU.mult)
                    link(ins)
                nxt = segment_of(BASE[segment] + SIZE[segment])

                def body(it, last):
                    for slot in range(2):
                        n = BASE[segment] + 2 * it + slot
                        if not (last and slot):
                            split_lo(n + 1, width(segment), 1 - slot)
                        elif nxt:
                            split_lo(n + 1, width(nxt), 1 - slot)
                        if segment in MOD_BESIDE:
                            mod_half(MOD_BESIDE[segment] + it, slot)
                        residual(n, slot, 2 * it + slot, 1, FFN_T0[f])
                    if segment in MOD_BESIDE:
                        mod_collect(MOD_BESIDE[segment] + it)

                with dve.Fori(0, SIZE[segment] // 2 - 1) as it:
                    body(it, False)
                body(SIZE[segment] // 2 - 1, True)

            def rsqrt(k_norm):
                t0 = NORM_T0[k_norm]
                dve.wait_ge(std_ready, k_norm + 1)
                nc.vector.reciprocal(rstd[:, t0:T], std[:, t0:T]).then_inc(rstd_ready, 1)

            def norm(k_norm):
                t0 = NORM_T0[k_norm]
                g = (k_norm // 3) * 24 + (k_norm % 3) * KT
                dve.wait_ge(mod_ready, (col(k_norm, 1) + KT) // 4)
                for v in range(2):
                    ins = nc.vector.scalar_tensor_tensor(gain[:, v, :], modv[:, col(k_norm, 1):col(k_norm, 1) + KT, v], 1.0,
                                                         gains[:, g:g + KT], ALU.add, ALU.mult)
                ins.then_inc(gain_ready, 1)
                rsqrt(k_norm)
                for k in range(KT):
                    dve.wait_ge(normed_ready, KT * k_norm + k + 1)
                    link(nc.vector.tensor_copy(a_hi[:, k, t0:T], normed[:, k % 2, t0:T]))
                    nc.vector.tensor_tensor(a_lo[:, k, t0:T], normed[:, k % 2, t0:T], a_hi[:, k, t0:T].bitcast(F32),
                                            ALU.subtract).then_inc(a_ready, 1)

            def mixer0():
                S, R = s5_sem, ret_sem
                norm(1)
                dve.wait_ge(S["rows"], 64)
                nc.vector.tensor_copy(prow[:, 2, :].rearrange("p (g s) -> p g s", g=2),
                                      dtrow[:].rearrange("p (g a) -> p g a", a=1).broadcast_to([32, 2, 64]))
                nc.vector.tensor_copy(drow[:, 1, :].rearrange("p (s c) -> p s c", s=4),
                                      drow[:, 0:1, 0:32].broadcast_to([16, 4, 32])).then_inc(S["spread"], 1)
                for j in range(2):
                    split_lo(BASE["s5_in"] + j + 1, 2048, 1 - j)
                    dve.wait_ge(pe_done, BASE["s5_in"] + j + 1)
                    for q in range(2, 4):
                        for s in range(4):
                            if q == 3 and s == 3:
                                dve.wait_ge(S["us_act"], j + 1)
                            ins = nc.vector.tensor_copy(us[32 * s:32 * s + 32, 8 * j + q:8 * j + q + 5:4, :],
                                                        ps[j][32 * q:32 * q + 32, :, s::4])
                    ins.then_inc(ps_free[j], 1)

                dve.wait_ge(S["turned_rows"], 1)
                src = bank[2][:, 0:96].rearrange("p (a c) -> p a c", a=3)
                nc.vector.tensor_copy(skip[:], bank[2][:, 96:112])
                link(nc.vector.tensor_copy(pt[:, 0:3, :], src))

                def tt(o, a, b, op):
                    link(nc.vector.tensor_tensor(q_(o), q_(a), q_(b), op))

                def ts(o, a, s1, op1, s2=None, op2=ALU.bypass):
                    if s2 is None:
                        link(nc.vector.tensor_scalar(q_(o), q_(a), s1, None, op1))
                    else:
                        link(nc.vector.tensor_scalar(q_(o), q_(a), s1, s2, op1, op2))

                def nearest(o, a):
                    ts(o, a, MAGIC, ALU.add)
                    ts(o, o, MAGIC, ALU.subtract)

                mul, add, sub = ALU.mult, ALU.add, ALU.subtract
                ts("k", "ldt", float(1 / np.log(2)), mul)
                ts("k", "k", -127.0, ALU.max, 128.0, ALU.min)
                nearest("k", "k")
                ts("x0", "k", -LN2_HI, mul)
                tt("r", "ldt", "x0", add)
                ts("x0", "k", -LN2_LO, mul)
                tt("r", "r", "x0", add)
                nc.vector.tensor_scalar(q_("r"), q_("r"), -1.0, 1.0, ALU.max, ALU.min).then_inc(S["act"], 1)
                ts("k", "k", 127.0, add, float(2 ** 23), mul)
                link(nc.vector.tensor_copy(kint[:], q_("k")))
                dve.wait_ge(S["tanh"], 1)
                ts("x0", "t", 1.0, add)
                ts("x1", "t", -1.0, mul, 1.0, add)
                link(nc.vector.reciprocal(q_("x1"), q_("x1")))
                tt("x0", "x0", "x1", mul)
                link(nc.vector.tensor_tensor(q_("dt"), q_("x0"), kint[:].bitcast(F32), mul))
                ts("lre", "lre", -1e-4, ALU.min)
                tt("a", "lre", "dt", mul)
                tt("u", "lim", "dt", mul)
                ts("u", "u", float(1 / (2 * np.pi)), mul)
                nearest("x0", "u")
                nc.vector.tensor_tensor(q_("u"), q_("u"), q_("x0"), sub).then_inc(S["act"], 1)
                dve.wait_ge(S["tanh"], 2)
                dve.wait_ge(S["sin"], 2)
                ts("x1", "t", -1.0, mul, 1.0, add)
                link(nc.vector.reciprocal(q_("x1"), q_("x1")))
                tt("em1", "t", "x1", mul)
                ts("em1", "em1", 2.0, mul)
                ts("rad", "em1", 1.0, add)
                tt("cm1", "shalf", "shalf", mul)
                ts("cm1", "cm1", -2.0, mul)
                ts("cos", "cm1", 1.0, add)
                tt("nre", "em1", "cos", mul)
                tt("nre", "nre", "cm1", add)
                tt("l1i", "rad", "sin", mul)
                tt("l1r", "rad", "cos", mul)
                tt("x0", "lre", "lre", mul)
                tt("x1", "lim", "lim", mul)
                tt("x0", "x0", "x1", add)
                link(nc.vector.reciprocal(q_("x0"), q_("x0")))
                tt("x1", "nre", "lre", mul)
                tt("x2", "l1i", "lim", mul)
                tt("x1", "x1", "x2", add)
                tt("wre", "x1", "x0", mul)
                tt("x1", "l1i", "lre", mul)
                tt("x2", "nre", "lim", mul)
                tt("x1", "x1", "x2", sub)
                tt("wim", "x1", "x0", mul)

                def power(n, a, b):
                    tt("x0", f"l{a}r", f"l{b}r", mul)
                    tt("x1", f"l{a}i", f"l{b}i", mul)
                    tt(f"l{n}r", "x0", "x1", sub)
                    tt("x0", f"l{a}r", f"l{b}i", mul)
                    tt("x1", f"l{a}i", f"l{b}r", mul)
                    tt(f"l{n}i", "x0", "x1", add)

                power(2, 1, 1)
                power(3, 2, 1)
                power(4, 2, 2)
                tt("x0", "rad", "rad", mul)
                link(nc.vector.tensor_tensor(r4[:].rearrange("p d q -> p (d q)"), q_("x0"), q_("x0"), mul))
                nc.vector.memset(q_("l0r"), 1.0)
                link(nc.vector.memset(q_("l0i"), 0.0))
                for d in range(2):
                    def part(x, d=d):
                        return q_(x)[:, 16 * d:16 * d + 16]
                    for n in range(5):
                        at = n if d == 0 else 4 - n
                        nc.vector.tensor_copy(pows[:, 0, d, :, at], part(f"l{n}r"))
                        nc.vector.tensor_scalar(pows[:, 1, d, :, at], part(f"l{n}i"), -1.0, None, mul)
                        if n < 4:
                            at = 3 - n if d == 0 else n
                            nc.vector.tensor_copy(wpows[:, 0, d, :, at], part(f"l{n}r"))
                            nc.vector.tensor_copy(wpows[:, 1, d, :, at], part(f"l{n}i"))
                ts("u", "u", 4.0, mul)
                nearest("x0", "u")
                tt("u", "u", "x0", sub)
                flat_c, flat_s = [x[:].rearrange("p d q j -> p (d q) j") for x in (tcos, tsin)]
                for d in range(2):
                    at = slice(16 * d, 16 * d + 16)
                    step = const[:, C_STEP + d * P:C_STEP + d * P + P].rearrange("p (a j) -> p a j", a=1).broadcast_to([P, 16, P])
                    u = q_("u")[:, at].rearrange("p (c a) -> p c a", a=1).broadcast_to([P, 16, P])
                    ins = nc.vector.tensor_tensor(flat_s[:, at], step, u, mul)
                link(ins)
                link(nc.vector.tensor_scalar(flat_c, flat_s, MAGIC, None, add))
                link(nc.vector.tensor_scalar(flat_c, flat_c, MAGIC, None, sub))
                link(nc.vector.tensor_tensor(flat_s, flat_s, flat_c, sub))
                nc.vector.scalar_tensor_tensor(flat_c, flat_s, -1.0, flat_s, mul, ALU.max).then_inc(S["act"], 1)
                dve.wait_ge(S["loads"], 16 * 12)
                br, bi = [b_raw[:, n].rearrange("p d q k -> p (d q) k") for n in range(2)]
                w2 = [q_(x).rearrange("p (c a) -> p c a", a=1).broadcast_to([P, 32, 16]) for x in ("wre", "wim")]
                b4 = [bt[:, n, :].rearrange("p (c k) -> p c k", k=16) for n in range(4)]
                nc.vector.tensor_tensor(b4[0], br, w2[0], mul)
                nc.vector.tensor_tensor(b4[1], bi, w2[1], mul)
                nc.vector.tensor_tensor(b4[2], br, w2[1], mul)
                link(nc.vector.tensor_tensor(b4[3], bi, w2[0], mul))
                nc.vector.tensor_tensor(b_in[:, 0].rearrange("p d q k -> p (d q) k"), b4[0], b4[1], sub)
                link(nc.vector.tensor_tensor(b_in[:, 1].rearrange("p d q k -> p (d q) k"), b4[2], b4[3], add))
                dve.wait_ge(S["c_copied"], 4)
                nc.vector.memset(cp[:].rearrange("p a b c d -> p (a b c d)"), 0.0)
                nc.vector.memset(wb[:].rearrange("p a b c d e -> p (a b c d e)"), 0.0)
                nc.vector.memset(xs[:].rearrange("p a b -> p (a b)"), 0.0).then_inc(S["pads"], 1)
                dve.wait_ge(S["pads"], 1)

                def build_w(pair, slot):
                    def b(ri):
                        return b_in[:, ri, :, bass.ds(pair, 1), :].broadcast_to([P, 2, 4, 16])

                    def l(ri):
                        x = wpows[:, ri, :, bass.ds(pair, 1), :].rearrange("p d a n -> p d n a")
                        return x.broadcast_to([P, 2, 4, 16])
                    o = [prod[:, n, :].rearrange("p (d n k) -> p d n k", d=2, n=4) for n in range(4)]
                    for n, (x, z) in enumerate(((0, 0), (1, 1), (0, 1), (1, 0))):
                        ins = nc.vector.tensor_tensor(o[n], b(x), l(z), mul)
                    ins.then_inc(S["wprod"], 1)
                    dve.wait_ge(S["wprod"], pair + 1)
                    if not early(pair, 2):
                        dve.wait_ge(S["kmm"], pair - 1)
                    for ri, op in ((0, sub), (1, add)):
                        for g in range(2):
                            at = slice(64 * g, 64 * g + 64)
                            ins = nc.vector.tensor_tensor(wb[at, slot, :, ri, :, 16 * g:16 * g + 16],
                                                          o[2 * ri][at], o[2 * ri + 1][at], op)
                    ins.then_inc(S["w"], 1)

                def build_c(pair, slot):
                    if not early(pair, 2):
                        dve.wait_ge(S["y"], pair - 1)
                    c_products(nc.vector, pair, (0, 1)).then_inc(S["cprod"], 1)
                    dve.wait_ge(S["cprod"], pair + 1)
                    c_combine(nc.vector, pair, slot, 0, add).then_inc(S["cre"], 1)

                def rotate(pair, slot):
                    v = bank[1 + slot][:].rearrange("p (d r j) -> p d r j", d=2, r=2)
                    dve.wait_ge(S["v"], pair + 1)

                    def table(x):
                        return x[:, :, bass.ds(pair, 1), :].broadcast_to([P, 2, 2, P])
                    nc.vector.tensor_tensor(rot[:, 0], v, table(tcos), mul)
                    nc.vector.tensor_tensor(rot[:, 1], v[:, :, ::-1, :], table(tsin), mul).then_inc(S["rot"], 1)
                    dve.wait_ge(S["rot"], pair + 1)
                    nc.vector.tensor_tensor(rot[:, 0, :, 0, :], rot[:, 0, :, 0, :], rot[:, 1, :, 0, :], add)
                    nc.vector.tensor_tensor(rot[:, 0, :, 1, :], rot[:, 0, :, 1, :], rot[:, 1, :, 1, :], sub).then_inc(S["z"], 1)
                    dve.wait_ge(S["z"], pair + 1)
                    if not early(pair, 1):
                        dve.wait_ge(S["back"], pair)
                    for ri in range(2):
                        ins = nc.vector.tensor_tensor_scan(zs[:, 1, ri, 63::-1], r4[:, 1, bass.ds(pair, 1)].broadcast_to([P, 64]),
                                                           rot[:, 0, 1, ri, 63::-1], 0.0, mul, add)
                    ins.then_inc(S["half"], 1)
                    for ri in range(2):
                        nc.vector.tensor_tensor_scan(zs[:, 0, ri, :], r4[:, 0, bass.ds(pair, 1)].broadcast_to([P, P]),
                                                     rot[:, 0, 0, ri, :], 0.0, mul, add)
                    dve.wait_ge(S["half"], pair + 1)
                    for ri in range(2):
                        ins = nc.vector.tensor_tensor_scan(zs[:, 1, ri, 127:63:-1], r4[:, 1, bass.ds(pair, 1)].broadcast_to([P, 64]),
                                                           rot[:, 0, 1, ri, 127:63:-1], zs[:, 1, ri, 0:1], mul, add)
                    ins.then_inc(S["scan"], 1)

                def kernel_tile(pair, slot):
                    dve.wait_ge(S["kmm"], pair + 1)
                    if not early(pair, 2):
                        dve.wait_ge(S["y"], pair - 1)
                    nc.vector.scalar_tensor_tensor(kt[:, slot, :], const[:, C_IDENT:C_IDENT + P], skip[:, bass.ds(pair, 1)],
                                                   ps_sum[:, 0:P], mul, add).then_inc(S["k"], 1)

                def pair_body(pair, slot, more):
                    if more:
                        build_w(pair + 1, 1 - slot)
                    kernel_tile(pair, slot)
                    rotate(pair, slot)
                    if more:
                        build_c(pair + 1, 1 - slot)

                build_w(0, 0)
                build_c(0, 0)
                pair_body(0, 0, True)
                pair_body(1, 1, True)
                with dve.Fori(1, 7) as it:
                    for slot in range(2):
                        pair_body(2 * it + slot, slot, True)
                pair_body(14, 0, True)
                pair_body(15, 1, False)

                base = BASE["ret_in"]
                for j in range(8):
                    split_lo(base + j + 1, 2048 if j < 7 else width("glu"), 1 - j % 2)
                    if 1 <= j < 5:
                        rope(j - 1, R)
                dve.wait_ge(R["loads"], 32)
                link(nc.vector.tensor_scalar(lg[:, 2, :], lgam[:], -1.0, None, mul))
                nc.vector.tensor_tensor(lg[:, 0, :], lgam[:], lg[:, 2, :], ALU.max).then_inc(R["gam"], 1)
                dve.wait_ge(R["exp1"], 2)
                link(nc.vector.tensor_scalar(lg[:, 0, :], lgam[:], 0.0, None, ALU.min))
                nc.vector.tensor_tensor(lg[:, 3, :], lg[:, 0, :], lg[:, 2, :], sub).then_inc(R["gam"], 1)
                dve.wait_ge(S["gelu"], 4)
                dve.wait_ge(pe_done, BASE["glu"])
                for m in range(4):
                    ins = nc.vector.tensor_copy(a_hi[:, 4 + m, :], y[:, m, :])
                link(ins)
                for m in range(4):
                    ins = nc.vector.tensor_tensor(a_lo[:, 4 + m, :], y[:, m, :], a_hi[:, 4 + m, :].bitcast(F32), sub)
                ins.then_inc(R["y_split"], 1)
                for hd in range(4):
                    dve.wait_ge(R["exp2"], hd + 1)
                    e = [ex[:, n, :].rearrange("p (t i) -> p t i", t=2) for n in range(4)]
                    nc.vector.tensor_tensor(ex[:, 0, :], ex[:, 0, :], lags[:, 1, :], mul)
                    link(nc.vector.tensor_tensor(ex[:, 1, :], ex[:, 1, :], lags[:, 3, :], mul))
                    nc.vector.tensor_tensor(decay[:, :, 0:256], e[0], e[1], add)
                    nc.vector.tensor_tensor(decay[:, :, 256:512], e[2], e[3], add).then_inc(R["mask"], 1)
                    dve.wait_ge(R["mask"], hd + 1)
                    dve.wait_ge(R["s"], hd + 1)
                    if hd:
                        dve.wait_ge(R["o"], hd)
                    for t in range(2):
                        nc.vector.scalar_tensor_tensor(scores[:, t, :], bank[t][:], KSCALE, decay[:, t, :], mul, mul)
                    nc.vector.scalar_tensor_tensor(scores[:, 2:4, 256:512], bank[2][:].rearrange("p (t i) -> p t i", t=2),
                                                   KSCALE, decay[:, :, 0:256], mul, mul).then_inc(R["p"], 1)
                    dve.wait_ge(R["std"], hd + 1)
                    link(nc.vector.reciprocal(rstd[:], std[:]))
                    link(nc.vector.tensor_tensor(rstd[:], rstd[:], gs[:, hd, :], mul))
                    link(nc.vector.tensor_tensor(normed[:, 0, :], rstd[:], ps_sum[:], mul))
                    link(nc.vector.tensor_copy(a_hi[:, hd, :], normed[:, 0, :]))
                    nc.vector.tensor_tensor(a_lo[:, hd, :], normed[:, 0, :], a_hi[:, hd, :].bitcast(F32), sub).then_inc(R["mix"], 1)
                for j in range(2):
                    split_lo(BASE["glu"] + j + 1, width("glu") if j == 0 else 2048, 1 - j)
                for j in range(2):
                    dve.wait_ge(ps_free[j], (BASE["glu"] + j) // 2 + 1)
                    for m in range(2 * j, 2 * j + 2):
                        ins = nc.vector.tensor_tensor(y[:, m, :], y[:, m, :], gs[:, m, :], mul)
                link(ins)
                for m in range(4):
                    link(nc.vector.tensor_copy(a_hi[:, 4 + m, :], y[:, m, :]))
                    nc.vector.tensor_tensor(a_lo[:, 4 + m, :], y[:, m, :], a_hi[:, 4 + m, :].bitcast(F32), sub).then_inc(R["mix"], 1)
                pair_down("ab_out", 1, 0)

            def rope(j, R):
                for m in range(2):
                    n = 2 * j + m
                    dve.wait_ge(R["swapped"], n + 1)
                    if n:
                        dve.wait_ge(R["rope"], n)
                    x = qk[:, n, NCTX:T]
                    nc.vector.tensor_tensor(ex[:, 0, 0:256], x, const[:, C_COS:C_COS + NLAT], ALU.mult)
                    link(nc.vector.tensor_tensor(ex[:, 1, 0:256], bank[n % 2][:, 0:256], const[:, C_SIN:C_SIN + NLAT], ALU.mult))
                    nc.vector.tensor_tensor(x, ex[:, 0, 0:256], ex[:, 1, 0:256], ALU.add).then_inc(R["rope"], 1)

            def pair_down(segment, k_norm, t0):
                nxt = segment_of(BASE[segment] + SIZE[segment])
                dve.wait_ge(mod_ready, (col(k_norm, 2) + KT) // 4)
                for v in range(2):
                    ins = nc.vector.tensor_copy(gate[:, v, :], modv[:, col(k_norm, 2):col(k_norm, 2) + KT, v])
                link(ins)
                for j in range(SIZE[segment]):
                    if j < SIZE[segment] - 1:
                        split_lo(BASE[segment] + j + 1, 2048, 1 - j % 2)
                    else:
                        split_lo(BASE[nxt], width(nxt), 0)
                    residual(BASE[segment] + j, j % 2, 2 * j, 2, t0)

            def mixer1():
                N = na_sem
                norm(4)
                b = bias[:].rearrange("p h r c -> p (h r) c")
                window = const[:, C_WINDOW:C_WINDOW + GRID_W].rearrange("p (a c) -> p a c", a=1).broadcast_to([P, 8, GRID_W])
                for x in range(12):
                    split_lo(BASE["na_q"] + x + 1, 2048, (x + 1) % 2)
                    if x == 0:
                        dve.wait_ge(N["bias"], 16 * 2 * NH)
                    nc.vector.tensor_tensor(b[:, 8 * x:8 * x + 8], b[:, 8 * x:8 * x + 8], window, ALU.min).then_inc(N["masked"], 1)

                def maxima(it, x):
                    it, x, u, s, head, _ = unit(it, x)
                    dve.wait_ge(N["s"], u + 1)
                    m = 2 - 2 * (x % 2)
                    local = ps[0][:, s, NCTX:T]
                    nc.vector.tensor_tensor(local, local, bias[:, bass.ds(head, 1), m:m + 4, :].rearrange("p a r c -> p (a r c)"),
                                            ALU.add).then_inc(N["added"], 1)
                    dve.wait_ge(N["added"], u + 1)
                    nc.vector.tensor_reduce(negmax[:, bass.ds(u, 1)], ps[0][:, s, :], AX.X, ALU.max,
                                            negate=True).then_inc(N["max"], 1)

                def diagonal(it, x):
                    it, x, u, s, _, _ = unit(it, x)
                    dve.wait_ge(N["exp"], u + 1)
                    nc.vector.reciprocal(recip[:, bass.ds(u, 1)], rowsum[:, bass.ds(u, 1)]).then_inc(N["recip"], 1)
                    dve.wait_ge(N["recip"], u + 1)
                    if not early(u, 2):
                        dve.wait_ge(N["turned"], u - 1)
                    nc.vector.tensor_scalar(diag[:, s, :], const[:, C_IDENT:C_IDENT + P], recip[:, bass.ds(u, 1)], None,
                                            ALU.mult).then_inc(N["diag"], 1)

                def step(it, x, more):
                    tile = unit(it, x)[5]
                    if more:
                        maxima(it, x + 2)
                        diagonal(it, x + 2)
                    if x % 4 == 3:
                        dve.wait_ge(N["hi"], tile + 1)
                        at = (slice(None), bass.ds(tile, 1), slice(NCTX, T))
                        nc.vector.tensor_tensor(
                            a_lo[at].rearrange("p a (r c) -> p (a r) c", c=GRID_W),
                            bank[x // 4][:, 0:NLAT].rearrange("p (r c) -> p r c", c=GRID_W)[:, :, ::-1],
                            a_hi[at].bitcast(F32).rearrange("p a (r c) -> p (a r) c", c=GRID_W),
                            ALU.subtract).then_inc(N["mix"], 1)

                def prologue():
                    dve.wait_ge(N["masked"], 12)
                    for x in range(2):
                        maxima(0, x)
                        diagonal(0, x)

                attention(dve, prologue, step)
                pair_down("na_out", 4, NCTX)

            nc.vector.memset(ones[:], 1.0).then_inc(set_done, 1)
            nc.vector.memset(half_pi[:], float(np.pi / 2))
            nc.vector.memset(eps[:], EPS).then_inc(set_done, 1)
            dve.wait_ge(rows_turned, 1)
            nc.vector.tensor_copy(bias_mod[:, 0:72], bank[2][:, 0:72])
            nc.vector.tensor_copy(gains[:], bank[2][:, 72:128])
            nc.vector.tensor_copy(bias_mod[:, 72:144], bank[2][:, 128:200]).then_inc(rows_copied, 1)
            nc.vector.tensor_copy(glu_b[:], bank[2][:, 216:220])
            nc.vector.tensor_copy(rows_t[:], bank[2][:, 200:216]).then_inc(rows_copied, 1)
            dve.wait_ge(cond_ready, 2)
            for s in range(FIRST_SUBS):
                mod_half(s, 0)
                mod_half(s, 1)
                mod_collect(s)
            split_lo(0, 2048, 0)
            for f in range(4):
                if f == 1:
                    mixer0()
                if f == 3:
                    mixer1()
                norm(NORM_OF[f])
                for b in range(2):
                    up(f"ffn{f}.up{b}")
                    down(f"ffn{f}.down{b}")
            rsqrt(6)
            dve.wait_ge(rstd_ready, 7)
            for k in range(KT):
                if k >= 2:
                    dve.wait_ge(out_turned, k - 1)
                link(nc.vector.tensor_tensor(normed[:, k % 2, NCTX:T], h[:, k, NCTX:T], rstd[:, NCTX:T], ALU.mult))
                nc.vector.tensor_scalar(scaled[:, k % 2, NCTX:T], normed[:, k % 2, NCTX:T],
                                        gains[:, 48 + k:49 + k], None, ALU.mult).then_inc(final_ready, 1)

        @block.gpsimd
        def _(pool):
            def norm(k_norm):
                t0 = NORM_T0[k_norm]
                pool.wait_ge(rstd_ready, k_norm + 1)
                for k in range(KT):
                    if KT * k_norm + k >= 2:
                        pool.wait_ge(normed_ready, KT * k_norm + k - 1)
                    nc.gpsimd.tensor_tensor(scaled[:, k % 2, t0:T], h[:, k, t0:T], rstd[:, t0:T],
                                            ALU.mult).then_inc(scaled_ready, 1)

            def up(segment):
                t0 = FFN_T0[int(segment[3])]
                with pool.Fori(0, SIZE[segment] // 2) as it:
                    for slot in range(2):
                        j = 2 * it + slot
                        pool.wait_ge(ps_free[slot], BASE[segment] // 2 + it + 1)
                        hi = g_hi[:, bass.ds(j, 1), t0:T].rearrange("p a t -> p (a t)")
                        lo = g_lo[:, bass.ds(j, 1), t0:T].rearrange("p a t -> p (a t)")
                        nc.gpsimd.tensor_copy(hi, gated[:, slot, t0:T]).then_inc(pool_hi, 1)
                        pool.wait_ge(pool_hi, g_base(segment) + j + 1)
                        nc.gpsimd.tensor_tensor(lo, gated[:, slot, t0:T], hi.bitcast(F32),
                                                ALU.subtract).then_inc(g_split, 1)

            def mixer0():
                S = s5_sem
                norm(1)
                pool.wait_ge(S["pads"], 1)
                pool.wait_ge(S["tables"], 2)

                def build_c(pair, slot):
                    if not early(pair, 2):
                        pool.wait_ge(S["y"], pair - 1)
                    c_products(nc.gpsimd, pair, (2, 3)).then_inc(S["cprod_im"], 1)
                    pool.wait_ge(S["cprod_im"], pair + 1)
                    c_combine(nc.gpsimd, pair, slot, 1, ALU.subtract).then_inc(S["cim"], 1)
                    pool.wait_ge(S["cim"], pair + 1)

                def turn_back(pair, slot):
                    pool.wait_ge(S["scan"], pair + 1)

                    def table(x):
                        return x[:, :, bass.ds(pair, 1), :].broadcast_to([P, 2, 2, P])
                    nc.gpsimd.tensor_tensor(back[:, 0], zs[:], table(tcos), ALU.mult)
                    nc.gpsimd.tensor_tensor(back[:, 1], zs[:, :, ::-1, :], table(tsin), ALU.mult).then_inc(S["back"], 1)
                    pool.wait_ge(S["back"], pair + 1)
                    flat = xs[:, slot]
                    x = flat[:, 1:2 * XS_D - 1].rearrange("p (d x) -> p d x", d=2)
                    for ri, op in ((0, ALU.subtract), (1, ALU.add)):
                        at, to = ri * P + 63, ri * 130 + 65
                        b = [back[:, n].rearrange("p d r j -> p (d r j)")[:, at:at + 194:193] for n in range(2)]
                        nc.gpsimd.tensor_tensor(flat[:, to:to + XS_D + 65:XS_D + 64], b[0], b[1], op)
                        x_to = x[:, :, ri * 130:ri * 130 + 130].rearrange("p d (b j) -> p d b j", b=2)[:, :, :, 0:64]
                        ins = nc.gpsimd.tensor_tensor(x_to, back[:, 0, :, ri, :], back[:, 1, :, ri, :], op)
                    ins.then_inc(S["x"], 1)

                build_c(0, 0)
                for pair in range(2):
                    build_c(pair + 1, 1 - pair)
                    turn_back(pair, pair)
                with pool.Fori(1, 7) as it:
                    for slot in range(2):
                        build_c(2 * it + slot + 1, 1 - slot)
                        turn_back(2 * it + slot, slot)
                build_c(15, 1)
                turn_back(14, 0)
                pool.wait_ge(S["y"], 14)
                turn_back(15, 1)

            def mixer1():
                norm(4)

            pool.wait_ge(set_done, 1)
            nc.gpsimd.memset(gated[:, 0, 0:1], 0.0).then_inc(g_split, 1)
            nc.gpsimd.memset(gated[:, 1, 0:1], 0.0).then_inc(g_split, 1)
            for f in range(4):
                if f == 1:
                    mixer0()
                if f == 3:
                    mixer1()
                norm(NORM_OF[f])
                for b in range(2):
                    up(f"ffn{f}.up{b}")

        @block.tensor
        def _(pe):
            def turn(dst, src, n=P):
                return pe.transpose(dst, src, const[0:n, C_IDENT:C_IDENT + n])

            def three(dst, w, x, start, stop_):
                pe.matmul(dst, w[0], x[1], start=start, stop=False)
                pe.matmul(dst, w[1], x[0], start=False, stop=False)
                return pe.matmul(dst, w[0], x[0], start=False, stop=stop_)

            def up(segment, first):
                t0 = FFN_T0[int(segment[3])]
                f = int(segment[3])

                def body(it, waits):
                    for slot in range(2):
                        pe.wait_ge(lo_ready, BASE[segment] + 2 * it + slot + 1)
                        if not early(BASE[segment] // 2 + it, 1):
                            pe.wait_ge(ps_free[slot], BASE[segment] // 2 + it)
                        w = [x[:, slot].rearrange("p (k h f) -> p k h f", k=KT, h=2) for x in (w_hi, w_lo)]
                        for k in range(KT):
                            if waits and slot == 0:
                                pe.wait_ge(a_ready, KT * NORM_OF[f] + k + 1)
                            for m in range(2):
                                mm = three(ps[slot][:, m, t0:T], [x[:, k, m] for x in w],
                                           (a_hi[:, k, t0:T], a_lo[:, k, t0:T]), k == 0, k == KT - 1)
                        mm.then_inc(pe_done, 1)
                    if segment in MOD_BESIDE:
                        mod_sum(MOD_BESIDE[segment] + it)

                if first:
                    body(0, True)
                with pe.Fori(1 if first else 0, SIZE[segment] // 2) as it:
                    body(it, False)

            def down(segment):
                f, b = int(segment[3]), int(segment[-1])
                t0, K = FFN_T0[f], BLOCKS[b]
                g_end = 2 + g_base(segment) + K
                with pe.Fori(0, SIZE[segment] // 2) as it:
                    for slot in range(2):
                        pe.wait_ge(lo_ready, BASE[segment] + 2 * it + slot + 1)
                        pe.wait_ge(ps_free[slot], BASE[segment] // 2 + it)
                        pe.wait_ge(g_split, g_end - 2)
                        w = [x[:, slot, 0:K * P].rearrange("p (k f) -> p k f", k=K) for x in (w_hi, w_lo)]
                        for k in range(K):
                            if k == K - 2:
                                pe.wait_ge(g_split, g_end)
                            mm = three(ps[slot][:, 0, t0:T], [x[:, k] for x in w],
                                       (g_hi[:, k, t0:T], g_lo[:, k, t0:T]), k == 0, k == K - 1)
                        mm.then_inc(pe_done, 1)
                    if segment in MOD_BESIDE:
                        mod_sum(MOD_BESIDE[segment] + it)

            def mod_sum(s):
                pe.wait_ge(mod_step, SUB_OPS * (s + 1))
                for m in range(4):
                    for v in range(2):
                        mm = pe.matmul(ps_mod[:, 2 * m + v:2 * m + v + 1], mod_acc[:, v, m * P:(m + 1) * P],
                                       ones[:, 0:1], start=True, stop=True)
                mm.then_inc(mod_summed, 1)

            def norm(k_norm):
                t0 = NORM_T0[k_norm]
                for k in range(KT):
                    pe.wait_ge(sq_ready, KT * k_norm + k + 1)
                    pe.matmul(ps_sum[:, t0:T], ones[:], sq[:, k % 2, t0:T], start=(k == 0),
                              stop=(k == KT - 1)).then_inc(sq_summed, 1)

            def mixer0():
                S, R = s5_sem, ret_sem
                norm(1)
                pe.wait_ge(S["spread"], 1)
                for n in range(3):
                    turn(bank[2][:, 32 * n:32 * n + 32], prow[:, n, :], 32)
                turn(bank[2][:, 96:112], drow[:, 1, :], 16).then_inc(S["turned_rows"], 1)
                for j in range(2):
                    pair_tile("s5_in", j, 8, 0, lambda k: pe.wait_ge(a_ready, KT + k + 1) if j == 0 else None)
                pe.wait_ge(S["loads"], 16 * 12)
                for ri in range(2):
                    for d in range(2):
                        if ri:
                            pe.wait_ge(S["c_copied"], d + 1)
                        for q in range(4):
                            mm = turn(bank[d][:, q * P:(q + 1) * P], crow[:, ri, d, q].rearrange("p a s -> p (a s)"))
                        mm.then_inc(S["c_turned"], 1)

                def turn_w(pair, slot):
                    pe.wait_ge(S["w"], pair + 1)
                    if not early(pair, 1):
                        pe.wait_ge(S["vt"], pair)
                    for n in range(4):
                        mm = turn(bank[0][:, n * P:(n + 1) * P],
                                  wb[:, slot].rearrange("p d r s c -> p (d r) (s c)")[:, n])
                    mm.then_inc(S["turned"], 1)

                def inputs_to_state(pair, slot):
                    pe.wait_ge(S["vt"], pair + 1)
                    if not early(pair, 2):
                        pe.wait_ge(S["rot"], pair - 1)
                    u = us[:, bass.ds(pair, 1), :].rearrange("p a j -> p (a j)")
                    v = bank[1 + slot]
                    for n in range(4):
                        mm = pe.matmul(v[:, n * P:(n + 1) * P], vt[:, slot, n, :], u, start=True, stop=True)
                    mm.then_inc(S["v"], 1)

                def kernel_products(pair, slot):
                    pe.wait_ge(S["cre"], pair + 1)
                    pe.wait_ge(S["cim"], pair + 1)
                    if not early(pair, 1):
                        pe.wait_ge(S["k"], pair)
                    for s in range(4):
                        o = ps_sum[32 * s:32 * s + 32, 0:P]
                        for d in range(2):
                            for ri in range(2):
                                lhs = wb[:, slot, d, ri, 3 if d == 0 else 0, :]
                                at = 3 - s if d == 0 else 8 + 4 - s
                                mm = pe.matmul(o, lhs, cp[:, slot, ri, at:at + 4, :].rearrange("p n c -> p (n c)"),
                                               start=(d == 0 and ri == 0), stop=(d == 1 and ri == 1))
                    mm.then_inc(S["kmm"], 1)

                def outputs(pair, slot, q, m):
                    pe.wait_ge(S["k"], pair + 1)
                    pe.wait_ge(S["x"], pair + 1)
                    u = us[:, bass.ds(pair, 1), :].rearrange("p a j -> p (a j)")
                    acc = ps[q // 2]

                    o = acc[:, q % 2, bass.ds(m * P, P)]
                    pe.matmul(o, kt[:, slot, :], u, start=True, stop=False)
                    for d in range(2):
                        for ri in range(2):
                            lhs = cp[:, slot, ri, 4 + 4 * d:8 + 4 * d, :].rearrange("p n c -> p (n c)")
                            x = xs[:, slot, XS_D * d + 130 * ri:XS_D * d + 130 * ri + 130].rearrange("p (b j) -> p b j", b=2)[:, :, d:d + 64]
                            mm = pe.matmul(o, lhs, x, start=False, stop=(d == 1 and ri == 1))
                    mm.then_inc(S["y"], 1)

                def pair_body(pair, slot, q, m, more):
                    kernel_products(pair, slot)
                    if more:
                        turn_w(pair + 1, 1 - slot)
                        inputs_to_state(pair + 1, 1 - slot)
                    outputs(pair, slot, q, m)

                pe.wait_ge(S["pads"], 1)
                for j in range(2):
                    pe.wait_ge(ps_free[j], BASE["s5_in"] // 2 + 1)
                turn_w(0, 0)
                inputs_to_state(0, 0)
                for q in range(4):
                    pair_body(q, q % 2, q, 0, True)
                with pe.Fori(1, 3) as it:
                    for q in range(4):
                        pair_body(4 * it + q, q % 2, q, it, True)
                for q in range(4):
                    pair_body(12 + q, q % 2, q, 3, q < 3)
                pe.wait_ge(S["gelu"], 4)
                for j in range(8):
                    if j in (4, 5):
                        value_tile("ret_in", j)
                    else:
                        pair_tile("ret_in", j, 8, 0)
                    if 1 <= j < 5:
                        for m in range(2):
                            n = 2 * (j - 1) + m
                            pe.wait_ge(ps_free[(j - 1) % 2], (BASE["ret_in"] + j - 1) // 2 + 1)
                            if n >= 2:
                                pe.wait_ge(R["rope"], n - 1)
                            pe.matmul(bank[n % 2][:, 0:256], const[:, C_SWAP:C_SWAP + P], qk[:, n, NCTX:T],
                                      start=True, stop=True).then_inc(R["swapped"], 1)
                pe.wait_ge(R["rope"], 8)
                for n in (6, 7):
                    pe.wait_ge(ps_free[n % 2], (BASE["ret_in"] + n) // 2 + 1)
                for hd in range(4):
                    if hd:
                        pe.wait_ge(R["p"], hd)
                    qh, kh = qk[:, hd, :], qk[:, 4 + hd, :]
                    if hd:
                        pe.wait_ge(R["std"], hd)
                    for t in range(2):
                        pe.matmul(bank[t][:], kh[:, t * P:(t + 1) * P], qh, start=True, stop=True)
                    for t in range(2):
                        mm = pe.matmul(bank[2][:, t * 256:(t + 1) * 256], kh[:, (2 + t) * P:(3 + t) * P], qh[:, 256:512],
                                       start=True, stop=True)
                    mm.then_inc(R["s"], 1)
                    pe.wait_ge(R["p"], hd + 1)
                    if hd:
                        pe.wait_ge(R["mix"], hd)
                    for t in (0, 2, 3, 1):
                        b = 0 if t < 2 else 256
                        mm = pe.matmul(ps_sum[:, b:512], vtok[:, t, hd * P:(hd + 1) * P], scores[:, t, b:512],
                                       start=(t == 0), stop=(t == 1))
                    mm.then_inc(R["o"], 1)
                    pe.wait_ge(R["osq"], hd + 1)
                    pe.matmul(bank[0][:], ones[:], sq[:, 0, :], start=True, stop=True).then_inc(R["sum"], 1)
                pe.wait_ge(R["y_split"], 1)
                for j in range(2):
                    pair_tile("glu", j, 4, 4)
                for j in range(4):
                    pair_tile("ab_out", j, 8, 0, lambda k: pe.wait_ge(R["mix"], k + 1) if j == 0 else None)

            def pair_tile(segment, j, K, at, before=None, t0=0, lat=False):
                n, slot = BASE[segment] + j, j % 2
                pe.wait_ge(lo_ready, n + 1)
                pe.wait_ge(ps_free[slot], n // 2)
                w = [x[:, slot, 0:K * 256].rearrange("p (k m f) -> p k m f", k=K, m=2) for x in (w_hi, w_lo)]
                for k in range(K):
                    if before:
                        before(k)
                    for m in range(2):
                        mm = three(ps[slot][:, m, t0:T], [x[:, k, m] for x in w],
                                   (a_hi[:, at + k, t0:T], a_lo[:, at + k, t0:T]), k == 0, k == K - 1)
                mm.then_inc(pe_done, 1)

            def value_tile(segment, j):
                n, slot = BASE[segment] + j, j % 2
                pe.wait_ge(lo_ready, n + 1)
                pe.wait_ge(ps_free[slot], n // 2)
                w = [x[:, slot].rearrange("p (k f) -> p k f", k=KT) for x in (w_hi, w_lo)]
                for t in range(4):
                    o = ps[slot][:, t // 2, (t % 2) * 256:(t % 2) * 256 + 256]
                    for k in range(KT):
                        mm = three(o, [x[:, k, t * P:(t + 1) * P] for x in (a_hi, a_lo)], [x[:, k] for x in w],
                                   k == 0, k == KT - 1)
                mm.then_inc(pe_done, 1)

            def mixer1():
                N = na_sem
                norm(4)
                for j in range(4):
                    pair_tile("na_q", j, 8, 0, lambda k: pe.wait_ge(a_ready, 4 * KT + k + 1) if j == 0 else None, NCTX)
                for j in range(4):
                    pair_tile("na_k", j, 8, 0)
                for j in range(4):
                    value_tile("na_v", j)
                for slot in range(2):
                    pe.wait_ge(ps_free[slot], (BASE["na_out"] + slot) // 2)

                def scores_of(it, x):
                    it, x, u, s, _, tile = unit(it, x)
                    if not early(u, 2):
                        pe.wait_ge(N["exp"], u - 1)
                    at = slice(64 * (x // 2 % 2), 64 * (x // 2 % 2) + 64)
                    pe.matmul(ps[0][:, s, :],
                              q_t[at, bass.ds(tile, 1), s * P:(s + 1) * P].rearrange("p a t -> p (a t)"),
                              k_t[at, bass.ds(tile, 1), :].rearrange("p a t -> p (a t)"),
                              start=True, stop=True).then_inc(N["s"], 1)

                def turn_probs(it, x):
                    it, x, u, s, _, _ = unit(it, x)
                    pe.wait_ge(N["diag"], u + 1)
                    for t in range(4):
                        mm = pe.matmul(ps[1][:, s, t * P:(t + 1) * P], prob[:, s, t * P:(t + 1) * P], diag[:, s, :],
                                       start=True, stop=True)
                    mm.then_inc(N["turned"], 1)

                def outputs_of(it, x):
                    it, x, u, s, head, tile = unit(it, x)
                    pe.wait_ge(N["copied"], u + 1)
                    if x % 4 == 0 and not early(tile, 2):
                        pe.wait_ge(N["mix"], tile - 1)
                    half = 64 * (x // 2 % 2)
                    for t in range(4):
                        mm = pe.matmul(bank[x // 4][half:half + 64, s * P:(s + 1) * P],
                                       v_tok[:, t, bass.ds(64 * head, 64)], prob_t[:, s, t * P:(t + 1) * P],
                                       start=(t == 0), stop=(t == 3))
                    mm.then_inc(N["o"], 1)

                def prologue():
                    scores_of(0, 0)
                    scores_of(0, 1)
                    turn_probs(0, 0)

                def step(it, x, more):
                    if more:
                        scores_of(it, x + 2)
                    outputs_of(it, x)
                    if more or x == 6:
                        turn_probs(it, x + 1)

                attention(nc.tensor, prologue, step)
                for j in range(4):
                    pair_tile("na_out", j, 8, 0, lambda k: pe.wait_ge(N["mix"], k + 1) if j == 0 else None, NCTX)

            pe.wait_ge(const_in, 16)
            pe.wait_ge(rows_in, 16 * 7)
            turn(bank[2][:, 0:128], rows[:, 0, :])
            turn(bank[2][:, 128:220], rows[0:92, 1, :], 92).then_inc(rows_turned, 1)
            pe.wait_ge(tokens_in, 32)
            for k in range(KT):
                if k >= 2:
                    pe.wait_ge(token_copied, k - 1)
                for t in range(4):
                    mm = turn(bank[k % 2][:, t * P:(t + 1) * P], tokens[:, t, k * P:(k + 1) * P])
                mm.then_inc(token_turned, 1)
            pe.wait_ge(set_done, 2)
            pe.wait_ge(rows_copied, 2)
            for s in range(FIRST_SUBS):
                mod_sum(s)
            for f in range(4):
                if f == 1:
                    mixer0()
                if f == 3:
                    mixer1()
                norm(NORM_OF[f])
                for b in range(2):
                    up(f"ffn{f}.up{b}", b == 0)
                    down(f"ffn{f}.down{b}")
            norm(6)
            for k in range(KT):
                pe.wait_ge(final_ready, k + 1)
                if k >= 2:
                    pe.wait_ge(out_copied, k - 1)
                for t in range(2):
                    mm = turn(bank[k % 2][:, t * P:(t + 1) * P], scaled[:, k % 2, NCTX + t * P:NCTX + (t + 1) * P])
                mm.then_inc(out_turned, 1)


INPUTS = ("x", "c", "ctx", "c_ctx", "w_mod", "b_mod", "norm_g", "ffn_w1", "ffn_w2", "w_in_ab", "w_out_ab",
          "ret_decay_logit", "s5_lam_re", "s5_lam_im", "s5_log_dt", "s5_b_re", "s5_b_im", "s5_c_re", "s5_c_im",
          "s5_d", "s5_glu_w", "s5_glu_b", "na_w_qkv", "na_w_o", "na_rpb", "final_g")


def kernel(**inputs):
    import concourse.bacc as bacc
    from concourse.bass_utils import run_bass_kernel_spmd

    nc = bacc.Bacc("TRN2", target_bir_lowering=False, num_devices=1)
    arrays = {f"in_{n}": np.ascontiguousarray(inputs[n]) for n in INPUTS}
    arrays["in_const"] = shape_constants()
    arrays["in_lags"] = shape_lags()
    aps = {n[3:]: nc.dram_tensor(n, a.shape, F32, kind="ExternalInput").ap() for n, a in arrays.items()}
    out = nc.dram_tensor("out", (1, NLAT, D), F32, kind="ExternalOutput").ap()
    program(nc, aps, out)
    return run_bass_kernel_spmd(nc, [arrays], core_ids=[0]).results[0]["out"]
```

```python
from contextlib import ExitStack

import numpy as np

import concourse.bass as bass
from concourse import mybir

F32 = mybir.dt.float32
F32R = mybir.dt.float32r
ALU = mybir.AluOpType
ACT = mybir.ActivationFunctionType
AX = mybir.AxisListType

P = 128
D = 1024
KT = D // P
NCTX = 256
NLAT = 256
T = NCTX + NLAT
HALVES = ((0, 0, NCTX), (1, NCTX, T))
FF = 2816
BLOCKS = (12, 10)
N_MOD = 9
GRID_W = 64
NH = 16
RELH, RELW = 15, 31
UNITS = 2 * NH
EPS = 1e-6
SUB = 512
SUBS = N_MOD * D // SUB
SUB_OPS = 2 * KT
FIRST_SUBS = 4

SEGMENTS = (
    [(f"ffn0.{s}", n) for s, n in (("up0", 12), ("down0", 8), ("up1", 10), ("down1", 8))]
    + [("s5_in", 2), ("ret_in", 8), ("glu", 2), ("ab_out", 4)]
    + [(f"ffn1.{s}", n) for s, n in (("up0", 12), ("down0", 8), ("up1", 10), ("down1", 8))]
    + [(f"ffn2.{s}", n) for s, n in (("up0", 12), ("down0", 8), ("up1", 10), ("down1", 8))]
    + [("na_q", 4), ("na_k", 4), ("na_v", 4), ("na_out", 4)]
    + [(f"ffn3.{s}", n) for s, n in (("up0", 12), ("down0", 8), ("up1", 10), ("down1", 8))]
)
BASE, SIZE, ORDER = {}, {}, []
_n = 0
for _name, _count in SEGMENTS:
    BASE[_name], SIZE[_name] = _n, _count
    ORDER.append(_name)
    _n += _count
TILES = _n

MOD_BESIDE = {"ffn0.up0": 4, "ffn0.down0": 10, "ffn0.up1": 14, "ffn1.up0": 19, "ffn1.up1": 25, "ffn2.up0": 30}

XS_D = 262
MAGIC = 1.5 * 2 ** 23
LN2_HI, LN2_LO = 0.693359375, -2.12194440e-4
TWO_PI = float(np.nextafter(np.float32(2 * np.pi), np.float32(0)))
KSCALE = float(P) ** -0.5
STATE = ("lre", "lim", "ldt", "k", "r", "t", "dt", "a", "u", "sin", "shalf", "em1", "rad", "cm1", "cos", "nre",
         "wre", "wim", "x0", "x1", "x2", "l0r", "l0i", "l1r", "l1i", "l2r", "l2i", "l3r", "l3i", "l4r", "l4i")

C_IDENT, C_SWAP, C_COS, C_SIN, C_STEP, C_WINDOW = 0, 128, 256, 512, 768, 1024
C_END = 1088


def shape_constants():
    c = np.zeros((P, C_END), np.float32)
    c[:, C_IDENT:C_IDENT + P] = np.eye(P)
    partner = np.arange(P) ^ 32
    c[partner, C_SWAP + np.arange(P)] = 1.0
    t = np.arange(NLAT)
    inv = (np.float32(10000.0) ** (-np.arange(0, 64, 2, dtype=np.float32) / np.float32(64))).astype(np.float32)
    for p in range(P):
        pos = (t // GRID_W if p < 64 else t % GRID_W).astype(np.float32)
        ang = (pos * inv[p % 32]).astype(np.float32)
        c[p, C_COS:C_COS + NLAT] = np.cos(ang)
        c[p, C_SIN:C_SIN + NLAT] = np.sin(ang) * (-1.0 if (p // 32) % 2 == 0 else 1.0)
    c[:, C_STEP:C_STEP + 2 * P] = np.concatenate(
        [np.arange(1, P + 1), np.arange(64, 0, -1), np.arange(P, 64, -1)])
    q = GRID_W - 1 - np.arange(P)[:, None] % GRID_W
    k = np.arange(GRID_W)[None, :]
    start = np.clip(q - 8, 0, GRID_W - 16)
    c[:, C_WINDOW:C_WINDOW + GRID_W] = np.where((k >= start) & (k < start + 16), 3e38, -1e30)
    return c


def shape_lags():
    j = (np.arange(2)[None, :, None] * P + np.arange(P)[:, None, None]).astype(np.float32)
    i = np.arange(256, dtype=np.float32)[None, None, :]
    d = i - j
    out = np.stack([np.maximum(d, 0), (d >= 0) * 1.0, np.maximum(-d, 0), (d <= 0) * 1.0, 256 + d, 256 - d], 1)
    return np.ascontiguousarray(out.reshape(P, 6 * 512).astype(np.float32))


def program(nc, i, out):
    with ExitStack() as ctx:
        def sem(name):
            return ctx.enter_context(nc.semaphore(name))

        def sbuf(name, shape, dt=F32, scope=ctx):
            return scope.enter_context(nc.sbuf_tensor(name, shape, dt))

        const = sbuf("const", [P, C_END])
        ones = sbuf("ones", [P, P])
        eps = sbuf("eps", [P, 1])
        h = sbuf("h", [P, KT, T])
        a_hi = sbuf("a_hi", [P, KT, T], F32R)
        a_lo = sbuf("a_lo", [P, KT, T], F32R)
        w_raw = sbuf("w_raw", [P, 2, 2048])
        w_hi = sbuf("w_hi", [P, 2, 2048], F32R)
        with ExitStack() as loop:
            cp = sbuf("cp", [P, 2, 2, 16, 32], F32, loop)
            wb = sbuf("wb", [P, 2, 2, 2, 4, 32], F32, loop)
            kt = sbuf("kt", [P, 2, P], F32, loop)
            prod = sbuf("prod", [P, 4, 128], F32, loop)
        w_lo = sbuf("w_lo", [P, 2, 2048], F32R)
        bias_mod = sbuf("bias_mod", [P, 2 * N_MOD * KT])
        gains = sbuf("gains", [P, 56])
        cond = sbuf("cond", [P, KT, 2])
        glu_b = sbuf("glu_b", [P, 4])
        half_pi = sbuf("half_pi", [P, 1])
        warm = sbuf("warm", [P, 1])
        rows_t = sbuf("rows_t", [P, 16])
        modv = sbuf("modv", [P, 2 * N_MOD * KT, 2])
        gain = sbuf("gain", [P, 2, KT])
        sq = sbuf("sq", [P, 2, T])
        sq_acc = sbuf("sq_acc", [P, T])
        std = sbuf("std", [P, T])
        rstd = sbuf("rstd", [P, T])
        scaled = sbuf("scaled", [P, 2, T])
        normed = sbuf("normed", [P, 2, T])
        gate = sbuf("gate", [P, 2, KT])

        ps_all = ctx.enter_context(nc.psum_tensor("ps_all", [P, 4, 512], F32))
        ps = [ps_all[:, 2 * n:2 * n + 2] for n in range(2)]
        bank = [ctx.enter_context(nc.psum_tensor(f"bank{n}", [P, 512], F32)) for n in range(4)]
        ps_mod, ps_sum = bank[2], bank[3]

        with ExitStack() as ffn:
            g_hi = sbuf("g_hi", [P, BLOCKS[0], T], F32R, ffn)
            g_lo = sbuf("g_lo", [P, BLOCKS[0], T], F32R, ffn)
            sil = sbuf("sil", [P, 2, T], F32, ffn)
            gated = sbuf("gated", [P, 2, T], F32, ffn)
            with ExitStack() as mod:
                mod_raw = sbuf("mod_raw", [P, 2, KT // 2, SUB], F32, mod)
                mod_acc = sbuf("mod_acc", [P, 2, SUB], F32, mod)
            bias = sbuf("bias", [P, NH, 6, GRID_W], F32, ffn)
        with ExitStack() as start:
            tokens = sbuf("tokens", [P, 4, D], F32, start)
            rows = sbuf("rows", [P, 2, P], F32, start)
            start_raw = sbuf("start_raw", [P, FIRST_SUBS, KT, SUB], F32, start)
            start_acc = sbuf("start_acc", [P, 2, SUB], F32, start)

        with ExitStack() as end:
            out_rows = sbuf("out_rows", [P, 2, D], F32, end)
        with ExitStack() as even:
            us = sbuf("us", [P, 16, P], F32, even)
            qk = sbuf("qk", [P, 8, T], F32, even)
            vtok = sbuf("vtok", [P, 4, 512], F32, even)
            with ExitStack() as s5:
                with ExitStack() as prep:
                    b_raw = sbuf("b_raw", [P, 2, 2, 16, 16], F32, prep)
                    crow = sbuf("crow", [P, 2, 2, 4, 2, 64], F32, prep)
                    bt = sbuf("bt", [P, 4, 512], F32, prep)
                    drow = sbuf("drow", [16, 2, P], F32, prep)
                tcos = sbuf("tcos", [P, 2, 16, P], F32, s5)
                tsin = sbuf("tsin", [P, 2, 16, P], F32, s5)
                b_in = sbuf("b_in", [P, 2, 2, 16, 16], F32, s5)
                c_in = sbuf("c_in", [P, 2, 2, 16, 16], F32, s5)
                pows = sbuf("pows", [P, 2, 2, 16, 5], F32, s5)
                wpows = sbuf("wpows", [P, 2, 2, 16, 4], F32, s5)
                r4 = sbuf("r4", [P, 2, 16], F32, s5)
                skip = sbuf("skip", [P, 16], F32, s5)
                with ExitStack() as scalars:
                    pt = sbuf("pt", [P, 32, 32], F32, scalars)
                    kint = sbuf("kint", [P, 32], mybir.dt.int32, scalars)
                    prow = sbuf("prow", [32, 3, P], F32, scalars)
                    dtrow = sbuf("dtrow", [32, 2], F32, scalars)
                cprod = sbuf("cprod", [P, 4, 160], F32, s5)
                xs = sbuf("xs", [P, 2, 2 * XS_D], F32, s5)
            with ExitStack() as ret:
                gs = sbuf("gs", [P, 4, T], F32, ret)
                lags = sbuf("lags", [P, 6, 512], F32, ret)
                lgam = sbuf("lgam", [P, 8], F32, ret)
                lg = sbuf("lg", [P, 4, 8], F32, ret)
                ex = sbuf("ex", [P, 4, 512], F32, ret)
                decay = sbuf("decay", [P, 2, T], F32, ret)
                scores = sbuf("scores", [P, 4, T], F32, ret)
                heads = sbuf("heads", [P, 4, T], F32, ret)
        y = us[:].rearrange("p (m q) j -> p m (q j)", m=4)
        with ExitStack() as na:
            q_t = sbuf("q_t", [P, KT, NLAT], F32, na)
            k_t = sbuf("k_t", [P, KT, T], F32, na)
            v_tok = sbuf("v_tok", [P, 4, D], F32, na)
            prob = sbuf("prob", [P, 2, T], F32, na)
            prob_t = sbuf("prob_t", [P, 2, T], F32, na)
            diag = sbuf("diag", [P, 2, P], F32, na)
            negmax = sbuf("negmax", [P, UNITS], F32, na)
            rowsum = sbuf("rowsum", [P, UNITS], F32, na)
            recip = sbuf("recip", [P, UNITS], F32, na)
        const_in, rows_in, tokens_in = sem("const_in"), sem("rows_in"), sem("tokens_in")
        set_done = sem("set_done")
        rows_turned, rows_copied = sem("rows_turned"), sem("rows_copied")
        cond_ready = sem("cond_ready")
        token_turned, token_copied = sem("token_turned"), sem("token_copied")
        w_in = [sem("w_in0"), sem("w_in1")]
        hi_ready, lo_ready = sem("hi_ready"), sem("lo_ready")
        pe_done = sem("pe_done")
        ps_free = [sem("ps_free0"), sem("ps_free1")]
        mod_in = [sem("mod_in0"), sem("mod_in1")]
        start_in = [sem(f"start_in{n}") for n in range(1, FIRST_SUBS)]
        start_step, start_product, start_copied = sem("start_step"), sem("start_product"), sem("start_copied")
        mod_step, mod_summed, mod_ready = sem("mod_step"), sem("mod_summed"), sem("mod_ready")
        sil_ready, g_split = sem("sil_ready"), sem("g_split")
        sq_ready, sq_summed = sem("sq_ready"), sem("sq_summed")
        std_ready, rstd_ready, scaled_ready = sem("std_ready"), sem("rstd_ready"), sem("scaled_ready")
        normed_ready, a_ready, gain_ready = sem("normed_ready"), sem("a_ready"), sem("gain_ready")
        pool_hi = sem("pool_hi")
        dve_chain = sem("dve_chain")
        final_ready = sem("final_ready")
        s5_sem = {n: sem("s5_" + n) for n in (
            "rows", "bias", "pads", "loads", "spread", "turned_rows", "c_turned", "c_copied", "act", "tanh",
            "sin", "tables", "us_act", "wprod", "w", "cprod", "cre", "cprod_im", "cim", "turned", "kmm", "vt", "k", "v",
            "rot", "z", "half", "scan", "back", "back_sin", "x", "y", "gelu")}
        ret_sem = {n: sem("ret_" + n) for n in (
            "loads", "swapped", "rope", "exp1", "exp2", "gam", "mask", "s", "p", "o", "osq", "kept", "sum", "ln", "std",
            "y_split", "mix")}
        na_sem = {n: sem("na_" + n) for n in (
            "bias", "masked", "s", "added", "max", "exp", "recip", "diag", "turned", "copied", "o",
            "hi", "mix")}
        out_turned, out_copied, out_stored = sem("out_turned"), sem("out_copied"), sem("out_stored")

        NORM_OF = (0, 2, 3, 5)
        FFN_T0 = (0, 0, 0, NCTX)
        NORM_T0 = (0, 0, 0, 0, 0, NCTX, NCTX)

        def width(segment):
            if "down" in segment:
                return BLOCKS[int(segment[-1])] * P
            return 4 * 256 if segment == "glu" else 2048

        def g_base(segment):
            return 22 * int(segment[3]) + (BLOCKS[0] if segment.endswith("1") else 0)

        def segment_of(n):
            for s in ORDER:
                if BASE[s] <= n < BASE[s] + SIZE[s]:
                    return s
            return None

        def halves(t0):
            return [x for x in HALVES if x[1] >= t0]

        def col(norm, which):
            return (norm // 3) * N_MOD * KT + (3 * (norm % 3) + which) * KT

        NORM_BESIDE = {"ffn0.down1": 1, "ab_out": 2, "ffn1.down1": 3, "ffn2.down1": 4, "na_out": 5, "ffn3.down1": 6}

        def norm_first(norm):
            return 0 if norm == 0 else (KT - 1 if "down" in last_h_tile(norm) else KT - 2)

        def last_h_tile(norm):
            return {1: "ffn0.down1", 2: "ab_out", 3: "ffn1.down1", 4: "ffn2.down1", 5: "na_out", 6: "ffn3.down1"}[norm]

        start_row = normed[0:2, :, :]
        vt = sq[:].rearrange("p s (n j) -> p s n j", n=4)
        rot = scaled[:].rearrange("p n (d r j) -> p n d r j", d=2, r=2)
        back = normed[:].rearrange("p n (d r j) -> p n d r j", d=2, r=2)
        zs = std[:].rearrange("p (d r j) -> p d r j", d=2, r=2)

        block = ctx.enter_context(nc.Block())

        def early(value, n):
            return isinstance(value, int) and value < n

        def unit(it, x):
            it, x = it + x // 8, x % 8
            return it, x, 8 * it + x, x % 2, 4 * it + x // 2, 2 * it + x // 4

        score_bank = [ps_all[:, 0, :], ps_all[:, 1, :], bank[2][:, :], bank[3][:, :]]

        def attention(engine, prologue, step):
            prologue()
            if engine is nc.tensor:
                for u in range(UNITS):
                    step(u // 8, u % 8, u < UNITS - 2)
                return
            for x in range(8):
                step(0, x, True)
            with engine.Fori(1, UNITS // 8 - 1) as it:
                for x in range(8):
                    step(it, x, True)
            for x in range(8):
                step(UNITS // 8 - 1, x, x < 6)

        def q_(name):
            return pt[:, STATE.index(name), :]

        def c_products(engine, pair, which):
            for n in which:
                x, z = ((0, 0), (1, 1), (0, 1), (1, 0))[n]
                c = c_in[:, x, :, bass.ds(pair, 1), :].broadcast_to([P, 2, 5, 16])
                l = pows[:, z, :, bass.ds(pair, 1), :].rearrange("p d a n -> p d n a").broadcast_to([P, 2, 5, 16])
                ins = engine.tensor_tensor(cprod[:, n, :].rearrange("p (d n k) -> p d n k", d=2, n=5), c, l, ALU.mult)
            return ins

        def c_combine(engine, pair, slot, ri, op):
            for g in range(2):
                at = slice(64 * g, 64 * g + 64)
                ins = engine.tensor_tensor(cp[at, slot, ri, 3:13, 16 * g:16 * g + 16],
                                           cprod[at, 2 * ri, :].rearrange("p (n k) -> p n k", k=16),
                                           cprod[at, 2 * ri + 1, :].rearrange("p (n k) -> p n k", k=16), op)
            return ins

        def mixer_loads(sp, segment):
            if segment == "ret_in":
                sp.wait_ge(pe_done, BASE["s5_in"])
                sp.wait_ge(mod_ready, 19)
                for n, x in enumerate(("s5_lam_re", "s5_lam_im")):
                    sp.dma_start(prow[:, n, :], i[x][0].rearrange("d (q g) s -> (d q) (g s)", g=2)).then_inc(s5_sem["rows"], 16)
                sp.dma_start(dtrow[:], i["s5_log_dt"][0].rearrange("d (q g) -> (d q) g", g=2)).then_inc(s5_sem["rows"], 16)
                sp.dma_start(drow[:, 0, 0:32], i["s5_d"][0].rearrange("(q c) -> q c", c=32)).then_inc(s5_sem["rows"], 16)
                for n, x in enumerate(("s5_c_re", "s5_c_im")):
                    for dup in range(2):
                        sp.dma_start(crow[:, n, :, :, dup, :].rearrange("p d q s -> p (d q) s"),
                                     i[x][0].rearrange("d (q a) k s -> (a k) (d q) s", a=8)).then_inc(s5_sem["loads"], 16)
                for n, x in enumerate(("s5_b_re", "s5_b_im")):
                    for d in range(2):
                        src = i[x][0, d].rearrange("(q g) s k -> g s q k", g=2)
                        for g in range(2):
                            sp.dma_start(b_raw[64 * g:64 * g + 64, n, d], src[g]).then_inc(s5_sem["loads"], 16)
            if segment == "ffn2.up1":
                sp.wait_ge(mod_ready, 2 * SUBS)
                for hd in range(NH):
                    for b in range(2):
                        src = bass.AP(tensor=i["na_rpb"].tensor, offset=hd * RELH * RELW + (5 - b) * RELW - 48,
                                      ap=[[1, GRID_W], [RELW, 6], [1, GRID_W]])
                        sp.dma_start(bias[64 * b:64 * b + 64, hd], src).then_inc(na_sem["bias"], 16)
            if segment == "glu":
                sp.wait_ge(s5_sem["y"], 16)
                sp.dma_start(lags[:].rearrange("p a b -> p (a b)"), i["lags"]).then_inc(ret_sem["loads"], 16)
                sp.dma_start(lgam[:], i["ret_decay_logit"][0].rearrange("(a d) h -> a (d h)", a=1).broadcast_to([P, 8])
                             ).then_inc(ret_sem["loads"], 16)

        @block.sync
        def _(sp):
            sp.dma_start(const[:], i["const"]).then_inc(const_in, 16)
            sp.dma_start(rows[0:72, 0, :], i["b_mod"][0].rearrange("(r c) -> r c", c=P)).then_inc(rows_in, 16)
            sp.dma_start(rows[72:120, 0, :], i["norm_g"].rearrange("l n (r c) -> (l n r) c", c=P)).then_inc(rows_in, 16)
            sp.dma_start(rows[120:128, 0, :], i["final_g"].rearrange("(r c) -> r c", c=P)).then_inc(rows_in, 16)
            sp.dma_start(rows[0:72, 1, :], i["b_mod"][1].rearrange("(r c) -> r c", c=P)).then_inc(rows_in, 16)
            sp.dma_start(rows[72:80, 1, :], i["c_ctx"].rearrange("(r c) -> r c", c=P)).then_inc(rows_in, 16)
            sp.dma_start(rows[80:88, 1, :], i["c"][0].rearrange("(r c) -> r c", c=P)).then_inc(rows_in, 16)
            sp.dma_start(rows[88:92, 1, :], i["s5_glu_b"][0].rearrange("(r c) -> r c", c=P)).then_inc(rows_in, 16)

            def fetch_mod(s, layer):
                w = i["w_mod"][layer].rearrange("(k p) n -> p k n", p=P)
                cols = bass.ds((s - layer * SUBS) * SUB, SUB)
                for half in range(2):
                    def one(half=half):
                        sp.dma_start(mod_raw[:, half], w[:, 4 * half:4 * half + 4, cols]).then_inc(mod_in[half], 16)
                    yield half, one

            def fetch_mod_after(s, layer, half, one):
                if early(s, FIRST_SUBS + 1):
                    sp.wait_ge(mod_ready, FIRST_SUBS)
                else:
                    sp.wait_ge(mod_step, SUB_OPS * (s - 1 - FIRST_SUBS) + 8 * (half + 1))
                one()

            def fetch_weights(segment, j, slot, free):
                dst = w_raw[:, slot]
                if free is not None:
                    sp.wait_ge(lo_ready, free)
                if "up" in segment:
                    f, b = int(segment[3]), int(segment[-1])
                    w = i["ffn_w1"][f // 2, f % 2].rearrange("(k p) (h f) -> p k h f", p=P, h=2)
                    at = bass.ds((j + (BLOCKS[0] if b else 0)) * P, P)
                    d = dst.rearrange("p (k h f) -> p k h f", k=KT, h=2)
                    parts = [(d[:, :, x], w[:, :, x, at]) for x in range(2)]
                elif "down" in segment:
                    f, b = int(segment[3]), int(segment[-1])
                    k0, n = (BLOCKS[0] if b else 0), BLOCKS[b]
                    w = i["ffn_w2"][f // 2, f % 2].rearrange("(k p) d -> p k d", p=P)
                    at = bass.ds(j * P, P)
                    d = dst[:, 0:n * P].rearrange("p (k f) -> p k f", k=n)
                    parts = [(d[:, x:x + n // 2], w[:, k0 + x:k0 + x + n // 2, at]) for x in (0, n // 2)]
                else:
                    src, c0, n = {"s5_in": ("w_in_ab", 2048, 8), "ret_in": ("w_in_ab", 0, 8), "glu": ("s5_glu_w", 0, 4),
                                  "ab_out": ("w_out_ab", 0, 8), "na_q": ("na_w_qkv", 0, 8), "na_k": ("na_w_qkv", D, 8),
                                  "na_v": ("na_w_qkv", 2 * D, 8), "na_out": ("na_w_o", 0, 8)}[segment]
                    w = i[src][0].rearrange("(k p) n -> p k n", p=P)
                    at = bass.ds(j * 256 + c0, 256)
                    d = dst[:, 0:n * 256].rearrange("p (k f) -> p k f", k=n)
                    parts = [(d[:, x:x + n // 2], w[:, x:x + n // 2, at]) for x in (0, n // 2)]
                for d, s in parts:
                    sp.dma_start(d, s).then_inc(w_in[slot], 16)

            def body(segment, it, first=False, mod_at=None):
                piece = []
                if mod_at is not None:
                    s = it + MOD_BESIDE[segment]
                    layer = 1 if (s >= SUBS if isinstance(s, int) else MOD_BESIDE[segment] >= SUBS) else 0
                    piece = list(fetch_mod(s, layer))
                for slot in range(2):
                    fetch_weights(segment, 2 * it + slot, slot,
                                  None if first else BASE[segment] + 2 * it + slot - 1)
                    if piece:
                        fetch_mod_after(s, layer, *piece[slot])

            for s in range(FIRST_SUBS):
                for half in range(2):
                    w = i["w_mod"][0].rearrange("(k p) n -> p k n", p=P)[:, 4 * half:4 * half + 4, s * SUB:(s + 1) * SUB]
                    sp.dma_start(start_raw[:, s, 4 * half:4 * half + 4], w).then_inc(mod_in[half] if s == 0 else start_in[s - 1], 16)
                if s == 0:
                    x = i["ctx"][0].rearrange("(t p) d -> p t d", p=P)
                    y = i["x"][0].rearrange("(t p) d -> p t d", p=P)
                    sp.dma_start(tokens[:, 0:2], x).then_inc(tokens_in, 16)
                    sp.dma_start(tokens[:, 2:4], y).then_inc(tokens_in, 16)
            for segment in ORDER:
                mixer_loads(sp, segment)
                its = SIZE[segment] // 2
                mod = segment if segment in MOD_BESIDE else None
                first = segment == ORDER[0]
                lo, hi = 0, its
                if first:
                    body(segment, 0, True, mod)
                    lo = 1
                if segment == "ffn0.up1":
                    hi = its - 1
                if hi - lo > 1:
                    with sp.Fori(lo, hi) as it:
                        body(segment, it, False, mod)
                    lo = hi
                for it in range(lo, its):
                    body(segment, it, False, mod)
            sp.wait_ge(out_copied, KT)
            for t in range(2):
                sp.dma_start(out[0, t * P:(t + 1) * P, :], out_rows[:, t, :]).then_inc(out_stored, 16)
            sp.wait_ge(out_stored, 32)

        @block.scalar
        def _(act):
            def split_hi(n, size, slot):
                act.wait_ge(w_in[slot], 16 * (n + 2 - slot))
                if not early(n, 2):
                    act.wait_ge(pe_done, n - 1)
                nc.scalar.activation(w_hi[:, slot, 0:size], w_raw[:, slot, 0:size], ACT.Copy).then_inc(hi_ready, 1)

            def up(segment):
                t0 = FFN_T0[int(segment[3])]

                def body(it, last):
                    for slot in range(2):
                        n = BASE[segment] + 2 * it + slot
                        nxt = width(segment) if not (last and slot) else width(segment_of(BASE[segment] + SIZE[segment]))
                        split_hi(n + 1, nxt, 1 - slot)
                        act.wait_ge(pe_done, n + 1)
                        nc.scalar.activation(sil[:, slot, t0:T], ps[slot][:, 0, t0:T], ACT.Silu).then_inc(sil_ready, 1)

                first = 1 if BASE[segment] == 0 else 0
                if first:
                    body(0, False)
                with act.Fori(first, SIZE[segment] // 2 - 1) as it:
                    body(it, False)
                body(SIZE[segment] // 2 - 1, True)

            def square(k_norm, k, slot):
                t0 = NORM_T0[k_norm]
                if k_norm:
                    per = 1 if "down" in last_h_tile(k_norm) else 2
                    if per == 1:
                        n = (BASE[last_h_tile(k_norm)] + k - slot) // 2
                    else:
                        n = (BASE[last_h_tile(k_norm)] + k // 2) // 2
                    act.wait_ge(ps_free[slot if per == 1 else (k // 2) % 2], n + 1)
                else:
                    act.wait_ge(token_copied, k + 1)
                if not early(KT * k_norm + k, 2):
                    act.wait_ge(sq_summed, KT * k_norm + k - 1)
                nc.scalar.activation(sq[:, slot, t0:T], h[:, bass.ds(k, 1), t0:T].rearrange("p a t -> p (a t)"),
                                     ACT.Square).then_inc(sq_ready, 1)

            def down(segment):
                nxt = segment_of(BASE[segment] + SIZE[segment])
                k_norm = NORM_BESIDE.get(segment)
                tiles = SIZE[segment]

                def step(t, slot, first=False):
                    if not (isinstance(t, int) and t == tiles - 1):
                        split_hi(BASE[segment] + t + 1, width(segment), 1 - slot)
                    elif nxt:
                        split_hi(BASE[segment] + t + 1, width(nxt), 0)
                    if k_norm and not first:
                        if "down" in segment:
                            square(k_norm, t - 1, 1 - slot)
                        else:
                            for m in range(2):
                                square(k_norm, 2 * t - 2 + m, m)

                if "down" in segment:
                    step(0, 0, True)
                    step(1, 1)
                    with act.Fori(1, tiles // 2 - 1) as it:
                        for slot in range(2):
                            step(2 * it + slot, slot)
                    step(tiles - 2, 0)
                    step(tiles - 1, 1)
                else:
                    for t in range(tiles):
                        step(t, t % 2, t == 0)

            def norm(k_norm):
                t0 = NORM_T0[k_norm]
                for k in range(norm_first(k_norm), KT):
                    square(k_norm, k, k % 2)
                nc.scalar.activation(warm[:], eps[:], ACT.Ln)
                act.wait_ge(sq_summed, KT * (k_norm + 1))
                nc.scalar.activation(std[:, t0:T], ps_sum[:, t0:T], ACT.Ln, bias=eps[:, 0:1],
                                     scale=1.0 / D).then_inc(std_ready, 1)
                act.wait_ge(std_ready, k_norm + 1)
                nc.scalar.activation(rstd[:, t0:T], std[:, t0:T], ACT.Exp, scale=-0.5).then_inc(rstd_ready, 1)
                if k_norm == 6:
                    return
                if k_norm == 0:
                    for s in range(2):
                        act.wait_ge(start_product, s + 1)
                        nc.scalar.activation(start_row[:, s, :], bank[s][0:2, :], ACT.Copy).then_inc(start_copied, 1)
                    act.wait_ge(w_in[0], 32)
                    nc.scalar.activation(w_hi[:, 0, :], w_raw[:, 0, :], ACT.Copy).then_inc(hi_ready, 1)
                act.wait_ge(gain_ready, k_norm + 1)
                for k in range(KT):
                    act.wait_ge(scaled_ready, KT * k_norm + k + 1)
                    if KT * k_norm + k >= 2:
                        act.wait_ge(a_ready, KT * k_norm + k - 1)
                    for half, b, e in halves(t0):
                        ins = nc.scalar.activation(normed[:, k % 2, b:e], scaled[:, k % 2, b:e], ACT.Identity,
                                                   bias=modv[:, col(k_norm, 0) + k, half:half + 1],
                                                   scale=gain[:, half, k:k + 1])
                    ins.then_inc(normed_ready, 1)

            def mixer0():
                S, R = s5_sem, ret_sem
                norm(1)
                for j in range(2):
                    split_hi(BASE["s5_in"] + j + 1, 2048, 1 - j)
                    act.wait_ge(pe_done, BASE["s5_in"] + j + 1)
                    for q in range(0, 2):
                        for s in range(4):
                            ins = nc.scalar.activation(
                                us[32 * s:32 * s + 32, 8 * j + q:8 * j + q + 5:4, :],
                                ps[j][32 * q:32 * q + 32, :, s::4], ACT.Copy)
                    ins.then_inc(S["us_act"], 1)
                act.wait_ge(S["act"], 1)
                nc.scalar.activation(q_("t"), q_("r"), ACT.Tanh, scale=0.5).then_inc(S["tanh"], 1)
                act.wait_ge(S["act"], 2)
                nc.scalar.activation(q_("t"), q_("a"), ACT.Tanh, scale=0.5).then_inc(S["tanh"], 1)
                nc.scalar.activation(q_("sin"), q_("u"), ACT.Sin, scale=TWO_PI).then_inc(S["sin"], 1)
                nc.scalar.activation(q_("shalf"), q_("u"), ACT.Sin, scale=TWO_PI / 2).then_inc(S["sin"], 1)
                base = BASE["ret_in"]

                def evacuate(j):
                    n = base + j
                    split_hi(n + 1, 2048 if j < 7 else width("glu"), 1 - j % 2)
                    act.wait_ge(pe_done, n + 1)
                    p = ps[j % 2]
                    if j < 4:
                        ins = nc.scalar.activation(qk[:, 2 * j:2 * j + 2, :], p[:, :, :], ACT.Copy)
                    elif j < 6:
                        ins = nc.scalar.activation(vtok[:, :, (j - 4) * 256:(j - 3) * 256],
                                                   p.rearrange("p a (b c) -> p (a b) c", b=2), ACT.Copy)
                    else:
                        ins = nc.scalar.activation(gs[:, 2 * j - 12:2 * j - 10, :], p[:, :, :], ACT.Silu)
                    ins.then_inc(ps_free[j % 2], 1)

                evacuate(0)
                evacuate(1)
                for ri in range(2):
                    for d in range(2):
                        act.wait_ge(S["c_turned"], 2 * ri + d + 1)
                        src = bank[d][:].rearrange("p (q g k) -> p q g k", q=16, g=2)
                        for g in range(2):
                            ins = nc.scalar.activation(c_in[64 * g:64 * g + 64, ri, d], src[64 * g:64 * g + 64, :, g, :],
                                                       ACT.Copy)
                        ins.then_inc(S["c_copied"], 1)
                for j in range(2, 5):
                    evacuate(j)
                act.wait_ge(S["act"], 3)
                nc.scalar.activation(tsin[:], tsin[:], ACT.Sin, scale=TWO_PI).then_inc(S["tables"], 1)
                nc.scalar.activation(tcos[:], tcos[:], ACT.Sin, bias=half_pi[:, 0:1], scale=-TWO_PI).then_inc(S["tables"], 1)
                evacuate(5)

                def turned(pair, slot):
                    act.wait_ge(S["turned"], pair + 1)
                    nc.scalar.activation(vt[:, slot].rearrange("p a b -> p (a b)"), bank[0][:], ACT.Copy).then_inc(S["vt"], 1)

                def gelu(m):
                    act.wait_ge(S["y"], 4 * m + 4)
                    for q in range(4):
                        for t in range(4):
                            ins = nc.scalar.activation(
                                y[32 * q:32 * q + 32, bass.ds(m, 1), t::4].rearrange("p a j -> p (a j)"),
                                ps_all[32 * t:32 * t + 32, bass.ds(m, 1), q * P:(q + 1) * P].rearrange("p a j -> p (a j)"),
                                ACT.Gelu_apprx_tanh)
                    ins.then_inc(S["gelu"], 1)

                turned(0, 0)
                for q in range(4):
                    turned(q + 1, (q + 1) % 2)
                with act.Fori(1, 3) as it:
                    turned(4 * it + 1, 1)
                    gelu(it - 1)
                    for q in range(1, 4):
                        turned(4 * it + q + 1, (q + 1) % 2)
                turned(13, 1)
                gelu(2)
                turned(14, 0)
                turned(15, 1)
                gelu(3)
                evacuate(6)
                evacuate(7)
                act.wait_ge(R["gam"], 1)
                nc.scalar.activation(lg[:, 1, :], lg[:, 0, :], ACT.Exp, scale=-1.0).then_inc(R["exp1"], 1)
                act.wait_ge(R["exp1"], 1)
                nc.scalar.activation(lg[:, 2, :], lg[:, 1, :], ACT.Ln, bias=ones[:, 0:1]).then_inc(R["exp1"], 1)
                act.wait_ge(R["gam"], 2)
                split_hi(BASE["glu"] + 1, width("glu"), 1)

                def exponentials(hd):
                    if hd:
                        act.wait_ge(R["mask"], hd)
                    for n, d in enumerate((0, 1, 0, 1)):
                        ins = nc.scalar.activation(ex[:, n, :], lags[:, (0, 2, 4, 5)[n], :], ACT.Exp,
                                                   scale=lg[:, 3, 4 * d + hd:4 * d + hd + 1])
                    ins.then_inc(R["exp2"], 1)

                exponentials(0)
                for hd in range(4):
                    if hd < 3:
                        exponentials(hd + 1)
                    act.wait_ge(R["o"], hd + 1)
                    if hd >= 2:
                        act.wait_ge(R["sum"], hd - 1)
                    nc.scalar.activation(sq[:, hd % 2, :], ps_sum[:], ACT.Square).then_inc(R["osq"], 1)
                    nc.scalar.activation(heads[:, hd, :], ps_sum[:], ACT.Copy).then_inc(R["kept"], 1)
                act.wait_ge(R["mask"], 4)
                for hd in range(4):
                    act.wait_ge(R["sum"], hd + 1)
                    nc.scalar.activation(ex[:, hd, :], ps_all[:, hd, :], ACT.Ln, bias=eps[:, 0:1], scale=1.0 / P).then_inc(R["ln"], 1)
                for hd in range(4):
                    act.wait_ge(R["ln"], hd + 1)
                    nc.scalar.activation(ex[:, hd, :], ex[:, hd, :], ACT.Exp, scale=-0.5).then_inc(R["std"], 1)
                act.wait_ge(R["mix"], 4)
                for j in range(2):
                    n = BASE["glu"] + j
                    if j:
                        split_hi(n + 1, 2048, 0)
                    act.wait_ge(pe_done, n + 1)
                    for m in range(2):
                        ins = nc.scalar.activation(gs[:, 2 * j + m, :], ps[j][:, m, :], ACT.Sigmoid,
                                                   bias=glu_b[:, 2 * j + m:2 * j + m + 1])
                    ins.then_inc(ps_free[j], 1)
                down("ab_out")

            def mixer1():
                N = na_sem
                norm(4)
                for segment in ("na_q", "na_k", "na_v"):
                    for j in range(4):
                        n = BASE[segment] + j
                        split_hi(n + 1, 2048, 1 - j % 2)
                        act.wait_ge(pe_done, n + 1)
                        p = ps[j % 2]
                        for m in range(2):
                            if segment == "na_q":
                                ins = nc.scalar.activation(
                                    q_t[:, 2 * j + m, :].rearrange("p (r c) -> p r c", c=GRID_W),
                                    p[:, m, NCTX:T].rearrange("p (r c) -> p r c", c=GRID_W)[:, :, ::-1],
                                    ACT.Copy, scale=0.125)
                            elif segment == "na_k":
                                ins = nc.scalar.activation(k_t[:, 2 * j + m, :], p[:, m, :], ACT.Copy)
                        if segment == "na_v":
                            ins = nc.scalar.activation(v_tok[:, :, j * 256:(j + 1) * 256],
                                                       p[:].rearrange("p a (b c) -> p (a b) c", b=2), ACT.Copy)
                        ins.then_inc(ps_free[j % 2], 1)

                def exps(it, x):
                    it, x, u, s, _, _ = unit(it, x)
                    act.wait_ge(N["max"], u + 1)
                    if not early(u, 2):
                        act.wait_ge(N["turned"], u - 1)
                    nc.scalar.activation(prob[:, s, :], score_bank[x % 4], ACT.Exp, bias=negmax[:, bass.ds(u, 1)],
                                         accum_out=rowsum[:, bass.ds(u, 1)]).then_inc(N["exp"], 1)

                def step(it, x, more):
                    _, _, u, s, _, tile = unit(it, x)
                    act.wait_ge(N["turned"], u + 1)
                    if not early(u, 2):
                        act.wait_ge(N["o"], u - 1)
                    nc.scalar.activation(prob_t[:, s, :], ps[1][:, s, :], ACT.Copy).then_inc(N["copied"], 1)
                    if more:
                        exps(it, x + 2)
                    if x % 4 == 3:
                        act.wait_ge(N["o"], u + 1)
                        nc.scalar.activation(
                            a_hi[:, bass.ds(tile, 1), NCTX:T].rearrange("p a (r c) -> p (a r) c", c=GRID_W),
                            bank[x // 4][:, 0:NLAT].rearrange("p (r c) -> p r c", c=GRID_W)[:, :, ::-1],
                            ACT.Copy).then_inc(N["hi"], 1)

                def prologue():
                    exps(0, 0)
                    exps(0, 1)

                attention(act, prologue, step)
                down("na_out")

            act.wait_ge(rows_copied, 2)
            nc.scalar.activation(cond[:, :, 0], rows_t[:, 0:KT], ACT.Silu).then_inc(cond_ready, 1)
            nc.scalar.activation(cond[:, :, 1], rows_t[:, KT:2 * KT], ACT.Silu).then_inc(cond_ready, 1)
            for k in range(KT):
                act.wait_ge(token_turned, k + 1)
                nc.scalar.activation(h[:, k, :], bank[k % 2][:, :], ACT.Copy).then_inc(token_copied, 1)
            act.wait_ge(set_done, 2)
            for f in range(4):
                if f == 1:
                    mixer0()
                if f == 3:
                    mixer1()
                norm(NORM_OF[f])
                for b in range(2):
                    up(f"ffn{f}.up{b}")
                    down(f"ffn{f}.down{b}")
            norm(6)
            for k in range(KT):
                act.wait_ge(out_turned, k + 1)
                nc.scalar.activation(out_rows[:, :, k * P:(k + 1) * P],
                                     bank[k % 2][:, 0:256].rearrange("p (t f) -> p t f", t=2),
                                     ACT.Copy).then_inc(out_copied, 1)

        @block.vector
        def _(dve):
            chain = [0]

            def link(ins):
                chain[0] += 1
                ins.then_inc(dve_chain, 1)
                dve.wait_ge(dve_chain, chain[0])

            def split_lo(n, size, slot):
                dve.wait_ge(hi_ready, n + 1)
                nc.vector.tensor_tensor(w_lo[:, slot, 0:size], w_raw[:, slot, 0:size],
                                        w_hi[:, slot, 0:size].bitcast(F32), ALU.subtract).then_inc(lo_ready, 1)

            def mod_half(s, half):
                dve.wait_ge(mod_in[half], 16 * (s + 2 - FIRST_SUBS))
                for k in range(4 * half, 4 * half + 4):
                    for v in range(2):
                        src, c = mod_raw[:, half, k % 4, :], cond[:, k, v:v + 1]
                        if k == 0:
                            ins = nc.vector.tensor_scalar(mod_acc[:, v, :], src, c, None, ALU.mult)
                        else:
                            dve.wait_ge(mod_step, SUB_OPS * (s - FIRST_SUBS) + 2 * k + v - 1)
                            ins = nc.vector.scalar_tensor_tensor(mod_acc[:, v, :], src, c, mod_acc[:, v, :],
                                                                 ALU.mult, ALU.add)
                        ins.then_inc(mod_step, 1)

            def mod_collect(s):
                dve.wait_ge(mod_summed, s + 1)
                at = bass.ds(4 * s, 4)
                nc.vector.tensor_tensor(modv[:, at, :], ps_mod[:, 0:8].rearrange("p (m v) -> p m v", v=2),
                                        bias_mod[:, at].rearrange("p (m a) -> p m a", a=1).broadcast_to([P, 4, 2]),
                                        ALU.add).then_inc(mod_ready, 1)

            def up(segment):
                t0 = FFN_T0[int(segment[3])]

                def body(it, last):
                    for slot in range(2):
                        n = BASE[segment] + 2 * it + slot
                        nxt = width(segment) if not (last and slot) else width(segment_of(BASE[segment] + SIZE[segment]))
                        if segment in MOD_BESIDE:
                            mod_half(MOD_BESIDE[segment] + it, slot)
                        split_lo(n + 1, nxt, 1 - slot)
                        dve.wait_ge(sil_ready, g_base(segment) + 2 * it + slot + 1)
                        dve.wait_ge(g_split, g_base(segment) + 2 * it + slot + 1)
                        nc.vector.tensor_tensor(gated[:, slot, t0:T], sil[:, slot, t0:T], ps[slot][:, 1, t0:T],
                                                ALU.mult).then_inc(ps_free[slot], 1)
                    if segment in MOD_BESIDE:
                        mod_collect(MOD_BESIDE[segment] + it)

                with dve.Fori(0, SIZE[segment] // 2 - 1) as it:
                    body(it, False)
                body(SIZE[segment] // 2 - 1, True)

            def residual(n, slot, at, pair, t0, gated_by=gate):
                dve.wait_ge(pe_done, n + 1)
                for m in range(pair):
                    for half, b, e in halves(t0):
                        ins = nc.vector.scalar_tensor_tensor(
                            h[:, bass.ds(at + m, 1), b:e].rearrange("p a t -> p (a t)"),
                            ps[slot][:, m, b:e], gated_by[:, half, bass.ds(at + m, 1)],
                            h[:, bass.ds(at + m, 1), b:e].rearrange("p a t -> p (a t)"), ALU.mult, ALU.add)
                ins.then_inc(ps_free[slot], 1)

            def down(segment):
                f, b = int(segment[3]), int(segment[-1])
                if b == 0:
                    dve.wait_ge(mod_ready, (col(NORM_OF[f], 2) + KT) // 4)
                    for v in range(2):
                        ins = nc.vector.tensor_scalar(gate[:, v, :], modv[:, col(NORM_OF[f], 2):col(NORM_OF[f], 2) + KT, v],
                                                      0.5, None, ALU.mult)
                    link(ins)
                nxt = segment_of(BASE[segment] + SIZE[segment])

                def body(it, last):
                    for slot in range(2):
                        n = BASE[segment] + 2 * it + slot
                        if segment in MOD_BESIDE:
                            mod_half(MOD_BESIDE[segment] + it, slot)
                        if not (last and slot):
                            split_lo(n + 1, width(segment), 1 - slot)
                        elif nxt:
                            split_lo(n + 1, width(nxt), 1 - slot)
                        residual(n, slot, 2 * it + slot, 1, FFN_T0[f])
                    if segment in MOD_BESIDE:
                        mod_collect(MOD_BESIDE[segment] + it)

                with dve.Fori(0, SIZE[segment] // 2 - 1) as it:
                    body(it, False)
                body(SIZE[segment] // 2 - 1, True)

            def norm(k_norm):
                t0 = NORM_T0[k_norm]
                g = (k_norm // 3) * 24 + (k_norm % 3) * KT
                dve.wait_ge(mod_ready, (col(k_norm, 1) + KT) // 4)
                for v in range(2):
                    ins = nc.vector.scalar_tensor_tensor(gain[:, v, :], modv[:, col(k_norm, 1):col(k_norm, 1) + KT, v], 1.0,
                                                         gains[:, g:g + KT], ALU.add, ALU.mult)
                ins.then_inc(gain_ready, 1)
                for k in range(KT):
                    dve.wait_ge(normed_ready, KT * k_norm + k + 1)
                    link(nc.vector.tensor_copy(a_hi[:, k, t0:T], normed[:, k % 2, t0:T]))
                    nc.vector.tensor_tensor(a_lo[:, k, t0:T], normed[:, k % 2, t0:T], a_hi[:, k, t0:T].bitcast(F32),
                                            ALU.subtract).then_inc(a_ready, 1)

            def mixer0():
                S, R = s5_sem, ret_sem
                norm(1)
                dve.wait_ge(S["rows"], 64)
                nc.vector.tensor_copy(prow[:, 2, :].rearrange("p (g s) -> p g s", g=2),
                                      dtrow[:].rearrange("p (g a) -> p g a", a=1).broadcast_to([32, 2, 64]))
                nc.vector.tensor_copy(drow[:, 1, :].rearrange("p (s c) -> p s c", s=4),
                                      drow[:, 0:1, 0:32].broadcast_to([16, 4, 32])).then_inc(S["spread"], 1)
                for j in range(2):
                    split_lo(BASE["s5_in"] + j + 1, 2048, 1 - j)
                    dve.wait_ge(pe_done, BASE["s5_in"] + j + 1)
                    for q in range(2, 4):
                        for s in range(4):
                            if q == 3 and s == 3:
                                dve.wait_ge(S["us_act"], j + 1)
                            ins = nc.vector.tensor_copy(us[32 * s:32 * s + 32, 8 * j + q:8 * j + q + 5:4, :],
                                                        ps[j][32 * q:32 * q + 32, :, s::4])
                    ins.then_inc(ps_free[j], 1)

                base = BASE["ret_in"]
                dve.wait_ge(S["turned_rows"], 1)
                src = bank[2][:, 0:96].rearrange("p (a c) -> p a c", a=3)
                nc.vector.tensor_copy(skip[:], bank[2][:, 96:112])
                link(nc.vector.tensor_copy(pt[:, 0:3, :], src))

                def tt(o, a, b, op):
                    link(nc.vector.tensor_tensor(q_(o), q_(a), q_(b), op))

                def ts(o, a, s1, op1, s2=None, op2=ALU.bypass):
                    if s2 is None:
                        link(nc.vector.tensor_scalar(q_(o), q_(a), s1, None, op1))
                    else:
                        link(nc.vector.tensor_scalar(q_(o), q_(a), s1, s2, op1, op2))

                def nearest(o, a):
                    ts(o, a, MAGIC, ALU.add)
                    ts(o, o, MAGIC, ALU.subtract)

                mul, add, sub = ALU.mult, ALU.add, ALU.subtract
                ts("k", "ldt", float(1 / np.log(2)), mul)
                ts("k", "k", -127.0, ALU.max, 128.0, ALU.min)
                nearest("k", "k")
                ts("x0", "k", -LN2_HI, mul)
                tt("r", "ldt", "x0", add)
                ts("x0", "k", -LN2_LO, mul)
                tt("r", "r", "x0", add)
                nc.vector.tensor_scalar(q_("r"), q_("r"), -1.0, 1.0, ALU.max, ALU.min).then_inc(S["act"], 1)
                ts("k", "k", 127.0, add, float(2 ** 23), mul)
                link(nc.vector.tensor_copy(kint[:], q_("k")))
                dve.wait_ge(S["tanh"], 1)
                ts("x0", "t", 1.0, add)
                ts("x1", "t", -1.0, mul, 1.0, add)
                link(nc.vector.reciprocal(q_("x1"), q_("x1")))
                tt("x0", "x0", "x1", mul)
                link(nc.vector.tensor_tensor(q_("dt"), q_("x0"), kint[:].bitcast(F32), mul))
                ts("lre", "lre", -1e-4, ALU.min)
                tt("a", "lre", "dt", mul)
                tt("u", "lim", "dt", mul)
                ts("u", "u", float(1 / (2 * np.pi)), mul)
                nearest("x0", "u")
                nc.vector.tensor_tensor(q_("u"), q_("u"), q_("x0"), sub).then_inc(S["act"], 1)
                dve.wait_ge(S["tanh"], 2)
                dve.wait_ge(S["sin"], 2)
                split_lo(base + 1, 2048, 1)
                ts("x1", "t", -1.0, mul, 1.0, add)
                link(nc.vector.reciprocal(q_("x1"), q_("x1")))
                tt("em1", "t", "x1", mul)
                ts("em1", "em1", 2.0, mul)
                ts("rad", "em1", 1.0, add)
                tt("cm1", "shalf", "shalf", mul)
                ts("cm1", "cm1", -2.0, mul)
                ts("cos", "cm1", 1.0, add)
                tt("nre", "em1", "cos", mul)
                tt("nre", "nre", "cm1", add)
                tt("l1i", "rad", "sin", mul)
                tt("l1r", "rad", "cos", mul)
                tt("x0", "lre", "lre", mul)
                tt("x1", "lim", "lim", mul)
                tt("x0", "x0", "x1", add)
                link(nc.vector.reciprocal(q_("x0"), q_("x0")))
                tt("x1", "nre", "lre", mul)
                tt("x2", "l1i", "lim", mul)
                tt("x1", "x1", "x2", add)
                tt("wre", "x1", "x0", mul)
                tt("x1", "l1i", "lre", mul)
                tt("x2", "nre", "lim", mul)
                tt("x1", "x1", "x2", sub)
                tt("wim", "x1", "x0", mul)

                def power(n, a, b):
                    tt("x0", f"l{a}r", f"l{b}r", mul)
                    tt("x1", f"l{a}i", f"l{b}i", mul)
                    tt(f"l{n}r", "x0", "x1", sub)
                    tt("x0", f"l{a}r", f"l{b}i", mul)
                    tt("x1", f"l{a}i", f"l{b}r", mul)
                    tt(f"l{n}i", "x0", "x1", add)

                power(2, 1, 1)
                power(3, 2, 1)
                power(4, 2, 2)
                tt("x0", "rad", "rad", mul)
                link(nc.vector.tensor_tensor(r4[:].rearrange("p d q -> p (d q)"), q_("x0"), q_("x0"), mul))
                nc.vector.memset(q_("l0r"), 1.0)
                link(nc.vector.memset(q_("l0i"), 0.0))
                for d in range(2):
                    def part(x, d=d):
                        return q_(x)[:, 16 * d:16 * d + 16]
                    for n in range(5):
                        at = n if d == 0 else 4 - n
                        nc.vector.tensor_copy(pows[:, 0, d, :, at], part(f"l{n}r"))
                        nc.vector.tensor_scalar(pows[:, 1, d, :, at], part(f"l{n}i"), -1.0, None, mul)
                        if n < 4:
                            at = 3 - n if d == 0 else n
                            nc.vector.tensor_copy(wpows[:, 0, d, :, at], part(f"l{n}r"))
                            nc.vector.tensor_copy(wpows[:, 1, d, :, at], part(f"l{n}i"))
                dve.wait_ge(S["loads"], 16 * 12)
                br, bi = [b_raw[:, n].rearrange("p d q k -> p (d q) k") for n in range(2)]
                w2 = [q_(x).rearrange("p (c a) -> p c a", a=1).broadcast_to([P, 32, 16]) for x in ("wre", "wim")]
                b4 = [bt[:, n, :].rearrange("p (c k) -> p c k", k=16) for n in range(4)]
                nc.vector.tensor_tensor(b4[0], br, w2[0], mul)
                nc.vector.tensor_tensor(b4[1], bi, w2[1], mul)
                nc.vector.tensor_tensor(b4[2], br, w2[1], mul)
                link(nc.vector.tensor_tensor(b4[3], bi, w2[0], mul))
                nc.vector.tensor_tensor(b_in[:, 0].rearrange("p d q k -> p (d q) k"), b4[0], b4[1], sub)
                link(nc.vector.tensor_tensor(b_in[:, 1].rearrange("p d q k -> p (d q) k"), b4[2], b4[3], add))
                ts("u", "u", 4.0, mul)
                nearest("x0", "u")
                tt("u", "u", "x0", sub)
                split_lo(base + 2, 2048, 0)
                rope(0, R)
                dve.wait_ge(S["c_copied"], 4)
                flat_c, flat_s = [x[:].rearrange("p d q j -> p (d q) j") for x in (tcos, tsin)]
                for d in range(2):
                    at = slice(16 * d, 16 * d + 16)
                    step = const[:, C_STEP + d * P:C_STEP + d * P + P].rearrange("p (a j) -> p a j", a=1).broadcast_to([P, 16, P])
                    u = q_("u")[:, at].rearrange("p (c a) -> p c a", a=1).broadcast_to([P, 16, P])
                    ins = nc.vector.tensor_tensor(flat_s[:, at], step, u, mul)
                link(ins)
                split_lo(base + 3, 2048, 1)
                rope(1, R)
                link(nc.vector.tensor_scalar(flat_c, flat_s, MAGIC, None, add))
                link(nc.vector.tensor_scalar(flat_c, flat_c, MAGIC, None, sub))
                split_lo(base + 4, 2048, 0)
                rope(2, R)
                link(nc.vector.tensor_tensor(flat_s, flat_s, flat_c, sub))
                nc.vector.scalar_tensor_tensor(flat_c, flat_s, -1.0, flat_s, mul, ALU.max).then_inc(S["act"], 1)
                split_lo(base + 5, 2048, 1)
                rope(3, R)
                link(nc.vector.memset(xs[:].rearrange("p a b -> p (a b)"), 0.0))
                dve.wait_ge(pe_done, base + 6)
                nc.vector.memset(cp[:].rearrange("p a b c d -> p (a b c d)"), 0.0)
                nc.vector.memset(wb[:].rearrange("p a b c d e -> p (a b c d e)"), 0.0).then_inc(S["pads"], 1)
                dve.wait_ge(S["pads"], 1)

                def build_w(pair, slot):
                    def b(ri):
                        return b_in[:, ri, :, bass.ds(pair, 1), :].broadcast_to([P, 2, 4, 16])

                    def l(ri):
                        x = wpows[:, ri, :, bass.ds(pair, 1), :].rearrange("p d a n -> p d n a")
                        return x.broadcast_to([P, 2, 4, 16])
                    o = [prod[:, n, :].rearrange("p (d n k) -> p d n k", d=2, n=4) for n in range(4)]
                    for n, (x, z) in enumerate(((0, 0), (1, 1), (0, 1), (1, 0))):
                        ins = nc.vector.tensor_tensor(o[n], b(x), l(z), mul)
                    ins.then_inc(S["wprod"], 1)
                    dve.wait_ge(S["wprod"], pair + 1)
                    if not early(pair, 2):
                        dve.wait_ge(S["kmm"], pair - 1)
                    for ri, op in ((0, sub), (1, add)):
                        for g in range(2):
                            at = slice(64 * g, 64 * g + 64)
                            ins = nc.vector.tensor_tensor(wb[at, slot, :, ri, :, 16 * g:16 * g + 16],
                                                          o[2 * ri][at], o[2 * ri + 1][at], op)
                    ins.then_inc(S["w"], 1)

                def build_c(pair, slot):
                    if not early(pair, 1):
                        dve.wait_ge(S["cre"], pair)
                    c_products(nc.vector, pair, (0, 1)).then_inc(S["cprod"], 1)
                    dve.wait_ge(S["cprod"], pair + 1)
                    if not early(pair, 2):
                        dve.wait_ge(S["y"], pair - 1)
                    c_combine(nc.vector, pair, slot, 0, add).then_inc(S["cre"], 1)

                def rotate(pair, slot):
                    v = bank[1 + slot][:].rearrange("p (d r j) -> p d r j", d=2, r=2)
                    dve.wait_ge(S["v"], pair + 1)

                    def table(x):
                        return x[:, :, bass.ds(pair, 1), :].broadcast_to([P, 2, 2, P])
                    nc.vector.tensor_tensor(rot[:, 0], v, table(tcos), mul)
                    nc.vector.tensor_tensor(rot[:, 1], v[:, :, ::-1, :], table(tsin), mul).then_inc(S["rot"], 1)
                    dve.wait_ge(S["rot"], pair + 1)
                    nc.vector.tensor_tensor(rot[:, 0, :, 0, :], rot[:, 0, :, 0, :], rot[:, 1, :, 0, :], add)
                    nc.vector.tensor_tensor(rot[:, 0, :, 1, :], rot[:, 0, :, 1, :], rot[:, 1, :, 1, :], sub).then_inc(S["z"], 1)
                    dve.wait_ge(S["z"], pair + 1)
                    if not early(pair, 1):
                        dve.wait_ge(S["back"], pair)
                    for ri in range(2):
                        ins = nc.vector.tensor_tensor_scan(zs[:, 1, ri, 63::-1], r4[:, 1, bass.ds(pair, 1)].broadcast_to([P, 64]),
                                                           rot[:, 0, 1, ri, 63::-1], 0.0, mul, add)
                    ins.then_inc(S["half"], 1)
                    for ri in range(2):
                        nc.vector.tensor_tensor_scan(zs[:, 0, ri, :], r4[:, 0, bass.ds(pair, 1)].broadcast_to([P, P]),
                                                     rot[:, 0, 0, ri, :], 0.0, mul, add)
                    dve.wait_ge(S["half"], pair + 1)
                    for ri in range(2):
                        ins = nc.vector.tensor_tensor_scan(zs[:, 1, ri, 127:63:-1], r4[:, 1, bass.ds(pair, 1)].broadcast_to([P, 64]),
                                                           rot[:, 0, 1, ri, 127:63:-1], zs[:, 1, ri, 0:1], mul, add)
                    ins.then_inc(S["scan"], 1)

                def turn_back_sine(pair):
                    dve.wait_ge(S["scan"], pair + 1)
                    if not early(pair, 1):
                        dve.wait_ge(S["x"], pair)
                    nc.vector.tensor_tensor(back[:, 1], zs[:, :, ::-1, :],
                                            tsin[:, :, bass.ds(pair, 1), :].broadcast_to([P, 2, 2, P]),
                                            mul).then_inc(S["back_sin"], 1)

                def kernel_tile(pair, slot):
                    dve.wait_ge(S["kmm"], pair + 1)
                    if not early(pair, 2):
                        dve.wait_ge(S["y"], pair - 1)
                    nc.vector.scalar_tensor_tensor(kt[:, slot, :], const[:, C_IDENT:C_IDENT + P], skip[:, bass.ds(pair, 1)],
                                                   ps_sum[:, 0:P], mul, add).then_inc(S["k"], 1)

                def pair_body(pair, slot, more):
                    if more:
                        build_w(pair + 1, 1 - slot)
                    kernel_tile(pair, slot)
                    rotate(pair, slot)
                    turn_back_sine(pair)
                    if more:
                        build_c(pair + 1, 1 - slot)

                build_w(0, 0)
                build_c(0, 0)
                pair_body(0, 0, True)
                pair_body(1, 1, True)
                with dve.Fori(1, 7) as it:
                    for slot in range(2):
                        pair_body(2 * it + slot, slot, True)
                pair_body(14, 0, True)
                pair_body(15, 1, False)

                dve.wait_ge(S["y"], 16)
                split_lo(base + 6, 2048, 0)
                split_lo(base + 7, 2048, 1)
                split_lo(base + 8, width("glu"), 0)
                dve.wait_ge(R["loads"], 32)
                link(nc.vector.tensor_scalar(lg[:, 2, :], lgam[:], -1.0, None, mul))
                nc.vector.tensor_tensor(lg[:, 0, :], lgam[:], lg[:, 2, :], ALU.max).then_inc(R["gam"], 1)
                dve.wait_ge(R["exp1"], 2)
                link(nc.vector.tensor_scalar(lg[:, 0, :], lgam[:], 0.0, None, ALU.min))
                nc.vector.tensor_tensor(lg[:, 3, :], lg[:, 0, :], lg[:, 2, :], sub).then_inc(R["gam"], 1)
                dve.wait_ge(S["gelu"], 4)
                dve.wait_ge(pe_done, BASE["glu"])
                for m in range(4):
                    ins = nc.vector.tensor_copy(a_hi[:, 4 + m, :], y[:, m, :])
                link(ins)
                for m in range(4):
                    ins = nc.vector.tensor_tensor(a_lo[:, 4 + m, :], y[:, m, :], a_hi[:, 4 + m, :].bitcast(F32), sub)
                ins.then_inc(R["y_split"], 1)
                split_lo(BASE["glu"] + 1, width("glu"), 1)

                def mask(hd):
                    dve.wait_ge(R["exp2"], hd + 1)
                    e = [ex[:, n, :].rearrange("p (t i) -> p t i", t=2) for n in range(4)]
                    nc.vector.tensor_tensor(ex[:, 0, :], ex[:, 0, :], lags[:, 1, :], mul)
                    link(nc.vector.tensor_tensor(ex[:, 1, :], ex[:, 1, :], lags[:, 3, :], mul))
                    nc.vector.tensor_tensor(decay[:, :, 0:256], e[0], e[1], add)
                    nc.vector.tensor_tensor(decay[:, :, 256:512], e[2], e[3], add).then_inc(R["mask"], 1)
                    dve.wait_ge(R["mask"], hd + 1)

                mask(0)
                for hd in range(4):
                    dve.wait_ge(R["s"], hd + 1)
                    if hd:
                        dve.wait_ge(R["o"], hd)
                    for t in range(2):
                        nc.vector.scalar_tensor_tensor(scores[:, t, :], bank[t][:], KSCALE, decay[:, t, :], mul, mul)
                    nc.vector.scalar_tensor_tensor(scores[:, 2:4, 256:512], bank[2][:].rearrange("p (t i) -> p t i", t=2),
                                                   KSCALE, decay[:, :, 0:256], mul, mul).then_inc(R["p"], 1)
                    dve.wait_ge(R["p"], hd + 1)
                    if hd < 3:
                        mask(hd + 1)
                dve.wait_ge(R["kept"], 4)
                for hd in range(4):
                    dve.wait_ge(R["std"], hd + 1)
                    link(nc.vector.tensor_tensor(heads[:, hd, :], heads[:, hd, :], gs[:, hd, :], mul))
                    link(nc.vector.tensor_tensor(heads[:, hd, :], heads[:, hd, :], ex[:, hd, :], mul))
                    link(nc.vector.tensor_copy(a_hi[:, hd, :], heads[:, hd, :]))
                    nc.vector.tensor_tensor(a_lo[:, hd, :], heads[:, hd, :], a_hi[:, hd, :].bitcast(F32), sub).then_inc(R["mix"], 1)
                split_lo(BASE["ab_out"], 2048, 0)
                for j in range(2):
                    dve.wait_ge(ps_free[j], (BASE["glu"] + j) // 2 + 1)
                    for m in range(2 * j, 2 * j + 2):
                        ins = nc.vector.tensor_tensor(y[:, m, :], y[:, m, :], gs[:, m, :], mul)
                link(ins)
                for m in range(4):
                    link(nc.vector.tensor_copy(a_hi[:, 4 + m, :], y[:, m, :]))
                    nc.vector.tensor_tensor(a_lo[:, 4 + m, :], y[:, m, :], a_hi[:, 4 + m, :].bitcast(F32), sub).then_inc(R["mix"], 1)
                pair_down("ab_out", 1, 0)

            def rope(j, R):
                for m in range(2):
                    n = 2 * j + m
                    dve.wait_ge(R["swapped"], n + 1)
                    if n:
                        dve.wait_ge(R["rope"], n)
                    x = qk[:, n, NCTX:T]
                    nc.vector.tensor_tensor(normed[:, 0, 0:256], x, const[:, C_COS:C_COS + NLAT], ALU.mult)
                    link(nc.vector.tensor_tensor(normed[:, 1, 0:256], bank[2 + n % 2][:, 0:256], const[:, C_SIN:C_SIN + NLAT], ALU.mult))
                    nc.vector.tensor_tensor(x, normed[:, 0, 0:256], normed[:, 1, 0:256], ALU.add).then_inc(R["rope"], 1)

            def pair_down(segment, k_norm, t0):
                nxt = segment_of(BASE[segment] + SIZE[segment])
                dve.wait_ge(mod_ready, (col(k_norm, 2) + KT) // 4)
                for v in range(2):
                    ins = nc.vector.tensor_copy(gate[:, v, :], modv[:, col(k_norm, 2):col(k_norm, 2) + KT, v])
                link(ins)
                for j in range(SIZE[segment]):
                    if j < SIZE[segment] - 1:
                        split_lo(BASE[segment] + j + 1, 2048, 1 - j % 2)
                    else:
                        split_lo(BASE[nxt], width(nxt), 0)
                    residual(BASE[segment] + j, j % 2, 2 * j, 2, t0)

            def mixer1():
                N = na_sem
                norm(4)
                b = bias[:].rearrange("p h r c -> p (h r) c")
                window = const[:, C_WINDOW:C_WINDOW + GRID_W].rearrange("p (a c) -> p a c", a=1).broadcast_to([P, 8, GRID_W])
                for x in range(12):
                    split_lo(BASE["na_q"] + x + 1, 2048, (x + 1) % 2)
                    if x == 0:
                        dve.wait_ge(N["bias"], 16 * 2 * NH)
                    nc.vector.tensor_tensor(b[:, 8 * x:8 * x + 8], b[:, 8 * x:8 * x + 8], window, ALU.min).then_inc(N["masked"], 1)

                def maxima(it, x):
                    it, x, u, s, head, _ = unit(it, x)
                    dve.wait_ge(N["s"], u + 1)
                    m = 2 - 2 * (x % 2)
                    local = score_bank[x % 4][:, NCTX:T]
                    nc.vector.tensor_tensor(local, local, bias[:, bass.ds(head, 1), m:m + 4, :].rearrange("p a r c -> p (a r c)"),
                                            ALU.add).then_inc(N["added"], 1)
                    dve.wait_ge(N["added"], u + 1)
                    nc.vector.tensor_reduce(negmax[:, bass.ds(u, 1)], score_bank[x % 4], AX.X, ALU.max,
                                            negate=True).then_inc(N["max"], 1)

                def diagonal(it, x):
                    it, x, u, s, _, _ = unit(it, x)
                    dve.wait_ge(N["exp"], u + 1)
                    nc.vector.reciprocal(recip[:, bass.ds(u, 1)], rowsum[:, bass.ds(u, 1)]).then_inc(N["recip"], 1)
                    dve.wait_ge(N["recip"], u + 1)
                    if not early(u, 2):
                        dve.wait_ge(N["turned"], u - 1)
                    nc.vector.tensor_scalar(diag[:, s, :], const[:, C_IDENT:C_IDENT + P], recip[:, bass.ds(u, 1)], None,
                                            ALU.mult).then_inc(N["diag"], 1)

                def step(it, x, more):
                    tile = unit(it, x)[5]
                    if more:
                        maxima(it, x + 2)
                        diagonal(it, x + 2)
                    if x % 4 == 3:
                        dve.wait_ge(N["hi"], tile + 1)
                        at = (slice(None), bass.ds(tile, 1), slice(NCTX, T))
                        nc.vector.tensor_tensor(
                            a_lo[at].rearrange("p a (r c) -> p (a r) c", c=GRID_W),
                            bank[x // 4][:, 0:NLAT].rearrange("p (r c) -> p r c", c=GRID_W)[:, :, ::-1],
                            a_hi[at].bitcast(F32).rearrange("p a (r c) -> p (a r) c", c=GRID_W),
                            ALU.subtract).then_inc(N["mix"], 1)

                def prologue():
                    dve.wait_ge(N["masked"], 12)
                    for x in range(2):
                        maxima(0, x)
                        diagonal(0, x)

                attention(dve, prologue, step)
                pair_down("na_out", 4, NCTX)

            nc.vector.memset(ones[:], 1.0).then_inc(set_done, 1)
            nc.vector.memset(eps[:], EPS).then_inc(set_done, 1)
            dve.wait_ge(rows_turned, 1)
            nc.vector.tensor_copy(bias_mod[:, 0:72], bank[2][:, 0:72])
            nc.vector.tensor_copy(gains[:], bank[2][:, 72:128])
            nc.vector.tensor_copy(bias_mod[:, 72:144], bank[2][:, 128:200]).then_inc(rows_copied, 1)
            nc.vector.tensor_copy(glu_b[:], bank[2][:, 216:220])
            nc.vector.tensor_copy(rows_t[:], bank[2][:, 200:216]).then_inc(rows_copied, 1)
            dve.wait_ge(cond_ready, 2)
            for s in range(2):
                for k in range(KT):
                    if s == 0 and k % 4 == 0:
                        dve.wait_ge(mod_in[k // 4], 16)
                    if s and k == 0:
                        dve.wait_ge(start_in[0], 32)
                    for v in range(2):
                        src, c = start_raw[:, s, k, :], cond[:, k, v:v + 1]
                        if k == 0:
                            ins = nc.vector.tensor_scalar(start_acc[:, v, :], src, c, None, ALU.mult)
                        else:
                            dve.wait_ge(start_step, SUB_OPS * s + 2 * k + v - 1)
                            ins = nc.vector.scalar_tensor_tensor(start_acc[:, v, :], src, c, start_acc[:, v, :],
                                                                 ALU.mult, ALU.add)
                        ins.then_inc(start_step, 1)
                mod_collect(s)
            for s in range(2, FIRST_SUBS):
                mod_collect(s)
            split_lo(0, 2048, 0)
            for f in range(4):
                if f == 1:
                    mixer0()
                if f == 3:
                    mixer1()
                norm(NORM_OF[f])
                for b in range(2):
                    up(f"ffn{f}.up{b}")
                    down(f"ffn{f}.down{b}")
            dve.wait_ge(rstd_ready, 7)
            for k in range(KT):
                if k >= 2:
                    dve.wait_ge(out_turned, k - 1)
                link(nc.vector.tensor_tensor(normed[:, k % 2, NCTX:T], h[:, k, NCTX:T], rstd[:, NCTX:T], ALU.mult))
                nc.vector.tensor_scalar(scaled[:, k % 2, NCTX:T], normed[:, k % 2, NCTX:T],
                                        gains[:, 48 + k:49 + k], None, ALU.mult).then_inc(final_ready, 1)

        @block.gpsimd
        def _(pool):
            def add_squares(k_norm):
                t0 = NORM_T0[k_norm]
                if k_norm:
                    pool.wait_ge(sq_summed, KT * k_norm)
                for k in range(1, KT - 1):
                    pool.wait_ge(sq_ready, KT * k_norm + k + 1)
                    if k > 1:
                        pool.wait_ge(sq_summed, KT * k_norm + k)
                    nc.gpsimd.tensor_tensor(sq_acc[:, t0:T], sq[:, 0, t0:T] if k == 1 else sq_acc[:, t0:T],
                                            sq[:, k % 2, t0:T], ALU.add).then_inc(sq_summed, 2 if k == 1 else 1)

            def norm(k_norm):
                t0 = NORM_T0[k_norm]
                add_squares(k_norm)
                pool.wait_ge(rstd_ready, k_norm + 1)
                for k in range(KT):
                    if KT * k_norm + k >= 2:
                        pool.wait_ge(normed_ready, KT * k_norm + k - 1)
                    nc.gpsimd.tensor_tensor(scaled[:, k % 2, t0:T], h[:, k, t0:T], rstd[:, t0:T],
                                            ALU.mult).then_inc(scaled_ready, 1)

            def up(segment):
                t0 = FFN_T0[int(segment[3])]
                with pool.Fori(0, SIZE[segment] // 2) as it:
                    for slot in range(2):
                        j = 2 * it + slot
                        pool.wait_ge(ps_free[slot], BASE[segment] // 2 + it + 1)
                        hi = g_hi[:, bass.ds(j, 1), t0:T].rearrange("p a t -> p (a t)")
                        lo = g_lo[:, bass.ds(j, 1), t0:T].rearrange("p a t -> p (a t)")
                        nc.gpsimd.tensor_copy(hi, gated[:, slot, t0:T]).then_inc(pool_hi, 1)
                        pool.wait_ge(pool_hi, g_base(segment) + j + 1)
                        nc.gpsimd.tensor_tensor(lo, gated[:, slot, t0:T], hi.bitcast(F32),
                                                ALU.subtract).then_inc(g_split, 1)

            def mixer0():
                S = s5_sem
                norm(1)
                pool.wait_ge(S["pads"], 1)
                pool.wait_ge(S["tables"], 2)

                def build_c(pair, slot):
                    c_products(nc.gpsimd, pair, (2, 3)).then_inc(S["cprod_im"], 1)
                    pool.wait_ge(S["cprod_im"], pair + 1)
                    if not early(pair, 2):
                        pool.wait_ge(S["y"], pair - 1)
                    c_combine(nc.gpsimd, pair, slot, 1, ALU.subtract).then_inc(S["cim"], 1)
                    pool.wait_ge(S["cim"], pair + 1)

                def turn_back(pair, slot):
                    pool.wait_ge(S["scan"], pair + 1)
                    if not early(pair, 1):
                        pool.wait_ge(S["x"], pair)

                    def table(x):
                        return x[:, :, bass.ds(pair, 1), :].broadcast_to([P, 2, 2, P])
                    nc.gpsimd.tensor_tensor(back[:, 0], zs[:], table(tcos), ALU.mult).then_inc(S["back"], 1)
                    pool.wait_ge(S["back"], pair + 1)
                    pool.wait_ge(S["back_sin"], pair + 1)
                    flat = xs[:, slot]
                    x = flat[:, 1:2 * XS_D - 1].rearrange("p (d x) -> p d x", d=2)
                    for ri, op in ((0, ALU.subtract), (1, ALU.add)):
                        at, to = ri * P + 63, ri * 130 + 65
                        b = [back[:, n].rearrange("p d r j -> p (d r j)")[:, at:at + 194:193] for n in range(2)]
                        nc.gpsimd.tensor_tensor(flat[:, to:to + XS_D + 65:XS_D + 64], b[0], b[1], op)
                        x_to = x[:, :, ri * 130:ri * 130 + 130].rearrange("p d (b j) -> p d b j", b=2)[:, :, :, 0:64]
                        ins = nc.gpsimd.tensor_tensor(x_to, back[:, 0, :, ri, :], back[:, 1, :, ri, :], op)
                    ins.then_inc(S["x"], 1)

                build_c(0, 0)
                for pair in range(2):
                    build_c(pair + 1, 1 - pair)
                    turn_back(pair, pair)
                with pool.Fori(1, 7) as it:
                    for slot in range(2):
                        build_c(2 * it + slot + 1, 1 - slot)
                        turn_back(2 * it + slot, slot)
                build_c(15, 1)
                turn_back(14, 0)
                pool.wait_ge(S["y"], 14)
                turn_back(15, 1)

            def mixer1():
                norm(4)

            nc.gpsimd.memset(half_pi[:], float(np.pi / 2)).then_inc(g_split, 2)
            for f in range(4):
                if f == 1:
                    mixer0()
                if f == 3:
                    mixer1()
                norm(NORM_OF[f])
                for b in range(2):
                    up(f"ffn{f}.up{b}")
            add_squares(6)

        @block.tensor
        def _(pe):
            def turn(dst, src, n=P):
                return pe.transpose(dst, src, const[0:n, C_IDENT:C_IDENT + n])

            def three(dst, w, x, start, stop_):
                pe.matmul(dst, w[0], x[1], start=start, stop=False)
                pe.matmul(dst, w[1], x[0], start=False, stop=False)
                return pe.matmul(dst, w[0], x[0], start=False, stop=stop_)

            def up(segment, first):
                t0 = FFN_T0[int(segment[3])]
                f = int(segment[3])

                def body(it, waits):
                    for slot in range(2):
                        pe.wait_ge(lo_ready, BASE[segment] + 2 * it + slot + 1)
                        if not early(BASE[segment] // 2 + it, 1):
                            pe.wait_ge(ps_free[slot], BASE[segment] // 2 + it)
                        w = [x[:, slot].rearrange("p (k h f) -> p k h f", k=KT, h=2) for x in (w_hi, w_lo)]
                        for k in range(KT):
                            if waits and slot == 0:
                                pe.wait_ge(a_ready, KT * NORM_OF[f] + k + 1)
                            for m in range(2):
                                mm = three(ps[slot][:, m, t0:T], [x[:, k, m] for x in w],
                                           (a_hi[:, k, t0:T], a_lo[:, k, t0:T]), k == 0, k == KT - 1)
                        mm.then_inc(pe_done, 1)
                    if segment in MOD_BESIDE:
                        mod_sum(MOD_BESIDE[segment] + it)

                if first:
                    body(0, True)
                with pe.Fori(1 if first else 0, SIZE[segment] // 2) as it:
                    body(it, False)

            def down(segment):
                f, b = int(segment[3]), int(segment[-1])
                t0, K = FFN_T0[f], BLOCKS[b]
                g_end = 2 + g_base(segment) + K
                with pe.Fori(0, SIZE[segment] // 2) as it:
                    for slot in range(2):
                        pe.wait_ge(lo_ready, BASE[segment] + 2 * it + slot + 1)
                        pe.wait_ge(ps_free[slot], BASE[segment] // 2 + it)
                        pe.wait_ge(g_split, g_end - 2)
                        w = [x[:, slot, 0:K * P].rearrange("p (k f) -> p k f", k=K) for x in (w_hi, w_lo)]
                        for k in range(K):
                            if k == K - 2:
                                pe.wait_ge(g_split, g_end)
                            mm = three(ps[slot][:, 0, t0:T], [x[:, k] for x in w],
                                       (g_hi[:, k, t0:T], g_lo[:, k, t0:T]), k == 0, k == K - 1)
                        mm.then_inc(pe_done, 1)
                    if segment in MOD_BESIDE:
                        mod_sum(MOD_BESIDE[segment] + it)

            def mod_sum(s):
                if early(s, FIRST_SUBS):
                    acc = start_acc
                    pe.wait_ge(start_step, SUB_OPS * (s + 1))
                else:
                    acc = mod_acc
                    pe.wait_ge(mod_step, SUB_OPS * (s + 1 - FIRST_SUBS))
                for m in range(4):
                    for v in range(2):
                        mm = pe.matmul(ps_mod[:, 2 * m + v:2 * m + v + 1], acc[:, v, m * P:(m + 1) * P],
                                       ones[:, 0:1], start=True, stop=True)
                mm.then_inc(mod_summed, 1)

            def norm(k_norm):
                t0 = NORM_T0[k_norm]
                pe.wait_ge(sq_summed, KT * k_norm + KT - 1)
                pe.matmul(ps_sum[:, t0:T], ones[:], sq_acc[:, t0:T], start=True, stop=False)
                pe.wait_ge(sq_ready, KT * k_norm + KT)
                pe.matmul(ps_sum[:, t0:T], ones[:], sq[:, (KT - 1) % 2, t0:T], start=False, stop=True).then_inc(sq_summed, 1)

            def mixer0():
                S, R = s5_sem, ret_sem
                norm(1)
                pe.wait_ge(S["spread"], 1)
                for n in range(3):
                    turn(bank[2][:, 32 * n:32 * n + 32], prow[:, n, :], 32)
                turn(bank[2][:, 96:112], drow[:, 1, :], 16).then_inc(S["turned_rows"], 1)
                for j in range(2):
                    pair_tile("s5_in", j, 8, 0, lambda k: pe.wait_ge(a_ready, KT + k + 1) if j == 0 else None)
                for j in range(6):
                    if j < 4:
                        pair_tile("ret_in", j, 8, 0)
                    else:
                        value_tile("ret_in", j)
                    if 1 <= j < 5:
                        pe.wait_ge(ps_free[(j - 1) % 2], (BASE["ret_in"] + j - 1) // 2 + 1)
                        for n in (2 * j - 2, 2 * j - 1):
                            if n >= 2:
                                pe.wait_ge(R["rope"], n - 1)
                            pe.matmul(bank[2 + n % 2][:, 0:256], const[:, C_SWAP:C_SWAP + P], qk[:, n, NCTX:T],
                                      start=True, stop=True).then_inc(R["swapped"], 1)
                    if j == 1:
                        pe.wait_ge(S["loads"], 16 * 12)
                        for ri in range(2):
                            for d in range(2):
                                if ri:
                                    pe.wait_ge(S["c_copied"], d + 1)
                                for q in range(4):
                                    mm = turn(bank[d][:, q * P:(q + 1) * P], crow[:, ri, d, q].rearrange("p a s -> p (a s)"))
                                mm.then_inc(S["c_turned"], 1)

                def turn_w(pair, slot):
                    pe.wait_ge(S["w"], pair + 1)
                    if not early(pair, 1):
                        pe.wait_ge(S["vt"], pair)
                    for n in range(4):
                        mm = turn(bank[0][:, n * P:(n + 1) * P],
                                  wb[:, slot].rearrange("p d r s c -> p (d r) (s c)")[:, n])
                    mm.then_inc(S["turned"], 1)

                def inputs_to_state(pair, slot):
                    pe.wait_ge(S["vt"], pair + 1)
                    if not early(pair, 2):
                        pe.wait_ge(S["rot"], pair - 1)
                    u = us[:, bass.ds(pair, 1), :].rearrange("p a j -> p (a j)")
                    v = bank[1 + slot]
                    for n in range(4):
                        mm = pe.matmul(v[:, n * P:(n + 1) * P], vt[:, slot, n, :], u, start=True, stop=True)
                    mm.then_inc(S["v"], 1)

                def kernel_products(pair, slot):
                    pe.wait_ge(S["cre"], pair + 1)
                    pe.wait_ge(S["cim"], pair + 1)
                    if not early(pair, 1):
                        pe.wait_ge(S["k"], pair)
                    for s in range(4):
                        wide = 0 if s < 2 else 1
                        for d, ri in ((wide, 0), (1 - wide, 0), (1 - wide, 1), (wide, 1)):
                            lhs = wb[:, slot, d, ri, 3 if d == 0 else 0, :]
                            at = 3 - s if d == 0 else 8 + 4 - s
                            a, b = (0, 4) if d == wide else ((s, 4) if d == 0 else (0, s + 1))
                            mm = pe.matmul(ps_sum[32 * s:32 * s + 32, 32 * a:32 * b], lhs,
                                           cp[:, slot, ri, at + a:at + b, :].rearrange("p n c -> p (n c)"),
                                           start=(d == wide and ri == 0), stop=(d == wide and ri == 1))
                    mm.then_inc(S["kmm"], 1)

                def outputs(pair, slot, q, m):
                    pe.wait_ge(S["k"], pair + 1)
                    pe.wait_ge(S["x"], pair + 1)
                    u = us[:, bass.ds(pair, 1), :].rearrange("p a j -> p (a j)")

                    o = ps_all[:, bass.ds(m, 1), q * P:(q + 1) * P].rearrange("p a j -> p (a j)")
                    pe.matmul(o, kt[:, slot, :], u, start=True, stop=False)
                    for d in range(2):
                        for ri in range(2):
                            lhs = cp[:, slot, ri, 4 + 4 * d:8 + 4 * d, :].rearrange("p n c -> p (n c)")
                            x = xs[:, slot, XS_D * d + 130 * ri:XS_D * d + 130 * ri + 130].rearrange("p (b j) -> p b j", b=2)[:, :, d:d + 64]
                            mm = pe.matmul(o, lhs, x, start=False, stop=(d == 1 and ri == 1))
                    mm.then_inc(S["y"], 1)

                def pair_body(it, q, more=True):
                    pair, slot = 4 * it + q, q % 2
                    kernel_products(pair, slot)
                    if q:
                        outputs(pair - 1, 1 - slot, q - 1, it)
                    elif not early(it, 1):
                        outputs(pair - 1, 1, 3, it - 1)
                    if more:
                        turn_w(pair + 1, 1 - slot)
                        inputs_to_state(pair + 1, 1 - slot)

                pe.wait_ge(S["pads"], 1)
                for j in (4, 5):
                    pe.wait_ge(ps_free[j % 2], (BASE["ret_in"] + j) // 2 + 1)
                pe.wait_ge(R["rope"], 8)
                turn_w(0, 0)
                inputs_to_state(0, 0)
                for q in range(4):
                    pair_body(0, q)
                with pe.Fori(1, 3) as it:
                    for q in range(4):
                        pair_body(it, q)
                for q in range(4):
                    pair_body(3, q, q < 3)
                outputs(15, 1, 3, 3)
                pe.wait_ge(S["gelu"], 4)
                for j in (6, 7):
                    pair_tile("ret_in", j, 8, 0)
                for n in (6, 7):
                    pe.wait_ge(ps_free[n % 2], (BASE["ret_in"] + n) // 2 + 1)

                def head_scores(hd):
                    if hd:
                        pe.wait_ge(R["p"], hd)
                    qh, kh = qk[:, hd, :], qk[:, 4 + hd, :]
                    for t in range(2):
                        pe.matmul(bank[t][:], kh[:, t * P:(t + 1) * P], qh, start=True, stop=True)
                    for t in range(2):
                        mm = pe.matmul(bank[2][:, t * 256:(t + 1) * 256], kh[:, (2 + t) * P:(3 + t) * P], qh[:, 256:512],
                                       start=True, stop=True)
                    mm.then_inc(R["s"], 1)

                def head_sum(hd):
                    pe.wait_ge(R["osq"], hd + 1)
                    pe.matmul(ps_all[:, hd, :], ones[:], sq[:, hd % 2, :], start=True, stop=True).then_inc(R["sum"], 1)

                head_scores(0)
                for hd in range(4):
                    pe.wait_ge(R["p"], hd + 1)
                    if hd < 3:
                        head_scores(hd + 1)
                    if hd:
                        pe.wait_ge(R["kept"], hd)
                    for t in (0, 2, 3, 1):
                        b = 0 if t < 2 else 256
                        mm = pe.matmul(ps_sum[:, b:512], vtok[:, t, hd * P:(hd + 1) * P], scores[:, t, b:512],
                                       start=(t == 0), stop=(t == 1))
                    mm.then_inc(R["o"], 1)
                    if hd:
                        head_sum(hd - 1)
                head_sum(3)
                pe.wait_ge(R["ln"], 4)
                pe.wait_ge(R["y_split"], 1)
                for j in range(2):
                    pair_tile("glu", j, 4, 4)
                for j in range(4):
                    pair_tile("ab_out", j, 8, 0, lambda k: pe.wait_ge(R["mix"], k + 1) if j == 0 else None)

            def pair_tile(segment, j, K, at, before=None, t0=0, lat=False):
                n, slot = BASE[segment] + j, j % 2
                pe.wait_ge(lo_ready, n + 1)
                pe.wait_ge(ps_free[slot], n // 2)
                w = [x[:, slot, 0:K * 256].rearrange("p (k m f) -> p k m f", k=K, m=2) for x in (w_hi, w_lo)]
                for k in range(K):
                    if before:
                        before(k)
                    for m in range(2):
                        mm = three(ps[slot][:, m, t0:T], [x[:, k, m] for x in w],
                                   (a_hi[:, at + k, t0:T], a_lo[:, at + k, t0:T]), k == 0, k == K - 1)
                mm.then_inc(pe_done, 1)

            def value_tile(segment, j):
                n, slot = BASE[segment] + j, j % 2
                pe.wait_ge(lo_ready, n + 1)
                pe.wait_ge(ps_free[slot], n // 2)
                w = [x[:, slot].rearrange("p (k f) -> p k f", k=KT) for x in (w_hi, w_lo)]
                for t in range(4):
                    o = ps[slot][:, t // 2, (t % 2) * 256:(t % 2) * 256 + 256]
                    for k in range(KT):
                        mm = three(o, [x[:, k, t * P:(t + 1) * P] for x in (a_hi, a_lo)], [x[:, k] for x in w],
                                   k == 0, k == KT - 1)
                mm.then_inc(pe_done, 1)

            def mixer1():
                N = na_sem
                norm(4)
                for j in range(4):
                    pair_tile("na_q", j, 8, 0, lambda k: pe.wait_ge(a_ready, 4 * KT + k + 1) if j == 0 else None, NCTX)
                for j in range(4):
                    pair_tile("na_k", j, 8, 0)
                for j in range(4):
                    value_tile("na_v", j)
                for slot in range(2):
                    pe.wait_ge(ps_free[slot], (BASE["na_out"] + slot) // 2)

                def scores_of(it, x):
                    it, x, u, s, _, tile = unit(it, x)
                    if not early(u, 4):
                        pe.wait_ge(N["exp"], u - 3)
                    at = slice(64 * (x // 2 % 2), 64 * (x // 2 % 2) + 64)
                    pe.matmul(score_bank[x % 4],
                              q_t[at, bass.ds(tile, 1), s * P:(s + 1) * P].rearrange("p a t -> p (a t)"),
                              k_t[at, bass.ds(tile, 1), :].rearrange("p a t -> p (a t)"),
                              start=True, stop=True).then_inc(N["s"], 1)

                def turn_probs(it, x):
                    it, x, u, s, _, _ = unit(it, x)
                    pe.wait_ge(N["diag"], u + 1)
                    for t in range(4):
                        mm = pe.matmul(ps[1][:, s, t * P:(t + 1) * P], prob[:, s, t * P:(t + 1) * P], diag[:, s, :],
                                       start=True, stop=True)
                    mm.then_inc(N["turned"], 1)

                def outputs_of(it, x):
                    it, x, u, s, head, tile = unit(it, x)
                    pe.wait_ge(N["copied"], u + 1)
                    if x % 4 == 0 and not early(tile, 2):
                        pe.wait_ge(N["mix"], tile - 1)
                    half = 64 * (x // 2 % 2)
                    for t in range(4):
                        mm = pe.matmul(bank[x // 4][half:half + 64, s * P:(s + 1) * P],
                                       v_tok[:, t, bass.ds(64 * head, 64)], prob_t[:, s, t * P:(t + 1) * P],
                                       start=(t == 0), stop=(t == 3))
                    mm.then_inc(N["o"], 1)

                def prologue():
                    scores_of(0, 0)
                    scores_of(0, 1)
                    scores_of(0, 2)
                    turn_probs(0, 0)

                def step(it, x, more):
                    if 8 * it + x + 3 < UNITS:
                        scores_of(it, x + 3)
                    outputs_of(it, x)
                    if more or x == 6:
                        turn_probs(it, x + 1)

                attention(nc.tensor, prologue, step)
                for j in range(4):
                    pair_tile("na_out", j, 8, 0, lambda k: pe.wait_ge(N["mix"], k + 1) if j == 0 else None, NCTX)

            pe.wait_ge(const_in, 16)
            pe.wait_ge(rows_in, 16 * 7)
            turn(bank[2][:, 0:128], rows[:, 0, :])
            turn(bank[2][:, 128:220], rows[0:92, 1, :], 92).then_inc(rows_turned, 1)
            pe.wait_ge(tokens_in, 32)
            for k in range(KT):
                if k >= 2:
                    pe.wait_ge(token_copied, k - 1)
                for t in range(4):
                    mm = turn(bank[k % 2][:, t * P:(t + 1) * P], tokens[:, t, k * P:(k + 1) * P])
                mm.then_inc(token_turned, 1)
            pe.wait_ge(set_done, 2)
            pe.wait_ge(rows_copied, 2)
            mod_sum(0)

            def product(s):
                pe.wait_ge(start_in[s - 1], 32)
                for k in range(KT):
                    mm = pe.matmul(bank[s - 2][0:2, :], cond[:, k, :], start_raw[:, s, k, :], start=(k == 0), stop=(k == KT - 1))
                mm.then_inc(start_product, 1)

            def turn_product(s):
                pe.wait_ge(start_copied, s - 1)
                pe.wait_ge(mod_ready, s)
                for m in range(4):
                    mm = turn(ps_mod[:, 2 * m:2 * m + 2], start_row[:, s - 2, m * P:(m + 1) * P], 2)
                mm.then_inc(mod_summed, 1)

            pe.wait_ge(token_copied, KT)
            product(2)
            norm(0)
            mod_sum(1)
            product(3)
            turn_product(2)
            turn_product(3)
            for f in range(4):
                if f == 1:
                    mixer0()
                if f == 3:
                    mixer1()
                if f:
                    norm(NORM_OF[f])
                for b in range(2):
                    up(f"ffn{f}.up{b}", b == 0)
                    down(f"ffn{f}.down{b}")
            norm(6)
            for k in range(KT):
                pe.wait_ge(final_ready, k + 1)
                if k >= 2:
                    pe.wait_ge(out_copied, k - 1)
                for t in range(2):
                    mm = turn(bank[k % 2][:, t * P:(t + 1) * P], scaled[:, k % 2, NCTX + t * P:NCTX + (t + 1) * P])
                mm.then_inc(out_turned, 1)


INPUTS = ("x", "c", "ctx", "c_ctx", "w_mod", "b_mod", "norm_g", "ffn_w1", "ffn_w2", "w_in_ab", "w_out_ab",
          "ret_decay_logit", "s5_lam_re", "s5_lam_im", "s5_log_dt", "s5_b_re", "s5_b_im", "s5_c_re", "s5_c_im",
          "s5_d", "s5_glu_w", "s5_glu_b", "na_w_qkv", "na_w_o", "na_rpb", "final_g")


def kernel(**inputs):
    import concourse.bacc as bacc
    from concourse.bass_utils import run_bass_kernel_spmd

    nc = bacc.Bacc("TRN2", target_bir_lowering=False, num_devices=1)
    arrays = {f"in_{n}": np.ascontiguousarray(inputs[n]) for n in INPUTS}
    arrays["in_const"] = shape_constants()
    arrays["in_lags"] = shape_lags()
    aps = {n[3:]: nc.dram_tensor(n, a.shape, F32, kind="ExternalInput").ap() for n, a in arrays.items()}
    out = nc.dram_tensor("out", (1, NLAT, D), F32, kind="ExternalOutput").ap()
    program(nc, aps, out)
    return run_bass_kernel_spmd(nc, [arrays], core_ids=[0]).results[0]["out"]
```
